# Optimizing a Trainium2 kernel written in Bass

```python
import jax, jax.numpy as jnp
from jax import lax
import numpy as np

D_MODEL = 1024
BATCH = 1
SEQ = 256
DEPTH = 1

N_ATTN_HEADS = 8
ATTN_HEAD_DIM = 64
ATTN_WIDTH = N_ATTN_HEADS * ATTN_HEAD_DIM
MOBA_BLOCK = 256
MOBA_TOPK = 3
Q_BLOCK = 128
GMLP_GROUPS = 8
GMLP_GROUP_DIM = 64
GMLP_WIDTH = GMLP_GROUPS * GMLP_GROUP_DIM
GMLP_CHUNK = 128
IN_SPLITS = (ATTN_WIDTH, 2 * ATTN_WIDTH, 3 * ATTN_WIDTH,
             3 * ATTN_WIDTH + GMLP_WIDTH, 3 * ATTN_WIDTH + 2 * GMLP_WIDTH,
             3 * ATTN_WIDTH + 2 * GMLP_WIDTH + D_MODEL)
IN_COLS = 3 * ATTN_WIDTH + 2 * GMLP_WIDTH + 2 * D_MODEL
PEER_HEADS = 8
PEER_N_KEYS = 128
PEER_N_EXPERTS = PEER_N_KEYS * PEER_N_KEYS
PEER_QUERY_DIM = 256
PEER_HALF = PEER_QUERY_DIM // 2
PEER_TOPK = 16
PEER_TOKEN_BLOCK = 128
ALPHA = float((2.0 * DEPTH) ** 0.25)
BETA = float((8.0 * DEPTH) ** -0.25)
LN_EPS = 1e-5

kernel_name = 'moba_gmlp_peer_deepnorm_adaln_block'

def _layernorm(x):
    xf = x.astype(jnp.float32)
    mu = xf.mean(-1, keepdims=True)
    var = jnp.square(xf - mu).mean(-1, keepdims=True)
    return ((xf - mu) * lax.rsqrt(var + LN_EPS)).astype(x.dtype)

def _alibi_slopes(n):
    return jnp.asarray([2.0 ** (-8.0 * (i + 1) / n) for i in range(n)], jnp.float32)

def _moba_attention(q, k, v):
    B, S, H, Dh = q.shape
    nb = -(-S // MOBA_BLOCK)
    pad = nb * MOBA_BLOCK - S
    kp = jnp.pad(k, ((0, 0), (0, pad), (0, 0), (0, 0)))
    vp = jnp.pad(v, ((0, 0), (0, pad), (0, 0), (0, 0)))
    kb = kp.reshape(B, nb, MOBA_BLOCK, H, Dh).transpose(0, 3, 1, 2, 4)
    vb = vp.reshape(B, nb, MOBA_BLOCK, H, Dh).transpose(0, 3, 1, 2, 4)
    kmean = kb.astype(jnp.float32).mean(axis=3)
    k_sel = min(MOBA_TOPK, nb)
    nq = S // Q_BLOCK
    qc = q.reshape(B, nq, Q_BLOCK, H, Dh).transpose(1, 0, 3, 2, 4)
    slopes = _alibi_slopes(H)
    scale = Dh ** -0.5
    gather_bh = jax.vmap(jax.vmap(lambda tab, idx: tab[idx]))

    def one_block(args):
        q_blk, ci = args
        t = ci * Q_BLOCK + jnp.arange(Q_BLOCK)
        own = (ci * Q_BLOCK) // MOBA_BLOCK
        gate = jnp.einsum('bhqd,bhnd->bhqn', q_blk.astype(jnp.float32), kmean)
        gate = jnp.where(jnp.arange(nb) < own, gate, -jnp.inf)
        _, sel = lax.top_k(gate, k_sel)
        sel_ok = sel < own
        k_g = gather_bh(kb, sel)
        v_g = gather_bh(vb, sel)
        s_sel = jnp.einsum('bhqd,bhqkld->bhqkl', q_blk, k_g).astype(jnp.float32) * scale
        pos_sel = sel[..., None] * MOBA_BLOCK + jnp.arange(MOBA_BLOCK)
        dist_sel = jnp.abs(t[None, None, :, None, None] - pos_sel).astype(jnp.float32)
        s_sel = s_sel - slopes[None, :, None, None, None] * dist_sel
        s_sel = jnp.where(sel_ok[..., None], s_sel, -jnp.inf)
        k_own = lax.dynamic_index_in_dim(kb, own, axis=2, keepdims=False)
        v_own = lax.dynamic_index_in_dim(vb, own, axis=2, keepdims=False)
        s_own = jnp.einsum('bhqd,bhld->bhql', q_blk, k_own).astype(jnp.float32) * scale
        diff = t[:, None] - (own * MOBA_BLOCK + jnp.arange(MOBA_BLOCK))[None, :]
        s_own = s_own - slopes[:, None, None] * jnp.abs(diff).astype(jnp.float32)
        s_own = jnp.where(diff >= 0, s_own, -jnp.inf)
        scores = jnp.concatenate([s_sel.reshape(B, H, Q_BLOCK, k_sel * MOBA_BLOCK), s_own], axis=-1)
        p = jax.nn.softmax(scores, axis=-1)
        p_sel = p[..., :k_sel * MOBA_BLOCK].reshape(B, H, Q_BLOCK, k_sel, MOBA_BLOCK).astype(v.dtype)
        p_own = p[..., k_sel * MOBA_BLOCK:].astype(v.dtype)
        return (jnp.einsum('bhqkl,bhqkld->bhqd', p_sel, v_g)
                + jnp.einsum('bhql,bhld->bhqd', p_own, v_own))

    out = lax.map(one_block, (qc, jnp.arange(nq)))
    return out.transpose(1, 0, 3, 2, 4).reshape(B, S, H * Dh)

def _chunked_sgu(gu, gv, sgu_ln_g, sgu_ln_b, w_spatial, b_spatial):
    B, S, _ = gu.shape
    u = jax.nn.gelu(gu, approximate=False)
    vv = jax.nn.gelu(gv, approximate=False).reshape(B, S, GMLP_GROUPS, GMLP_GROUP_DIM)
    vv = _layernorm(vv) * sgu_ln_g + sgu_ln_b
    nc = S // GMLP_CHUNK
    vv = vv.reshape(B, nc, GMLP_CHUNK, GMLP_GROUPS, GMLP_GROUP_DIM)
    mask = jnp.tril(jnp.ones((GMLP_CHUNK, GMLP_CHUNK), dtype=bool))
    w = jnp.where(mask, w_spatial, 0)
    sv = jnp.einsum('gts,bcsgd->bctgd', w, vv) + b_spatial.T[None, None, :, :, None]
    return u * sv.reshape(B, S, GMLP_WIDTH)

def _peer(h, w_peer_q, peer_sub_keys, peer_u, peer_v):
    B, S, D = h.shape
    q = (h @ w_peer_q).reshape(B, S, PEER_HEADS, 2, PEER_HALF)
    s = jnp.einsum('bshcd,hcnd->bshcn', q, peer_sub_keys).astype(jnp.float32)
    top_s, top_i = lax.top_k(s, PEER_TOPK)
    cand = (top_s[..., 0, :, None] + top_s[..., 1, None, :]).reshape(B, S, PEER_HEADS, PEER_TOPK * PEER_TOPK)
    cand_idx = (top_i[..., 0, :, None] * PEER_N_KEYS + top_i[..., 1, None, :]).reshape(B, S, PEER_HEADS, PEER_TOPK * PEER_TOPK)
    best_s, best_pos = lax.top_k(cand, PEER_TOPK)
    expert_idx = jnp.take_along_axis(cand_idx, best_pos, axis=-1)
    g = jax.nn.softmax(best_s, axis=-1).astype(h.dtype)
    nt = (B * S) // PEER_TOKEN_BLOCK
    e_per_tok = PEER_HEADS * PEER_TOPK
    hx = h.reshape(nt, PEER_TOKEN_BLOCK, D)
    ix = expert_idx.reshape(nt, PEER_TOKEN_BLOCK, e_per_tok)
    gx = g.reshape(nt, PEER_TOKEN_BLOCK, e_per_tok)

    def one(args):
        hb, ib, gb = args
        u = peer_u[ib]
        a = jax.nn.gelu(jnp.einsum('td,ted->te', hb, u), approximate=False)
        return jnp.einsum('te,ted->td', gb * a, peer_v[ib])

    return lax.map(one, (hx, ix, gx)).reshape(B, S, D)

def _modulate(x, shift, scale):
    return _layernorm(x) * (1 + scale[:, None, :]) + shift[:, None, :]

def setup_inputs(seed: int = 0) -> dict:
    key = jax.random.key(seed)
    ks = jax.random.split(key, 24)
    L, D = DEPTH, D_MODEL
    nrm = lambda k, shape, s: jax.random.normal(k, shape, jnp.float32) * s
    return {
        'x': nrm(ks[0], (BATCH, SEQ, D), 1.0),
        'c': nrm(ks[1], (BATCH, D), 1.0),
        'w_cond': nrm(ks[2], (L, D, 6 * D), 0.2 * D ** -0.5),
        'b_cond': nrm(ks[3], (L, 6 * D), 0.01),
        'w_in': nrm(ks[4], (L, D, IN_COLS), D ** -0.5),
        'w_attn_up': nrm(ks[5], (L, ATTN_WIDTH, D), ATTN_WIDTH ** -0.5),
        'w_gmlp_up': nrm(ks[6], (L, GMLP_WIDTH, D), GMLP_WIDTH ** -0.5),
        'w_out': nrm(ks[7], (L, D, D), BETA * D ** -0.5),
        'sgu_ln_g': 1.0 + nrm(ks[8], (L, GMLP_GROUPS, GMLP_GROUP_DIM), 0.02),
        'sgu_ln_b': nrm(ks[9], (L, GMLP_GROUPS, GMLP_GROUP_DIM), 0.02),
        'w_spatial': nrm(ks[10], (L, GMLP_GROUPS, GMLP_CHUNK, GMLP_CHUNK), 0.5 * GMLP_CHUNK ** -0.5),
        'b_spatial': 1.0 + nrm(ks[11], (L, GMLP_GROUPS, GMLP_CHUNK), 0.02),
        'ln1_g': 1.0 + nrm(ks[12], (L, D), 0.02),
        'ln1_b': nrm(ks[13], (L, D), 0.02),
        'w_peer_q': nrm(ks[14], (L, D, PEER_HEADS * PEER_QUERY_DIM), D ** -0.5),
        'peer_sub_keys': nrm(ks[15], (L, PEER_HEADS, 2, PEER_N_KEYS, PEER_HALF), PEER_HALF ** -0.5),
        'peer_u': nrm(ks[16], (L, PEER_N_EXPERTS, D), D ** -0.5),
        'peer_v': nrm(ks[17], (L, PEER_N_EXPERTS, D), BETA),
        'ln2_g': 1.0 + nrm(ks[18], (L, D), 0.02),
        'ln2_b': nrm(ks[19], (L, D), 0.02),
    }

def reference(x, c, w_cond, b_cond, w_in, w_attn_up, w_gmlp_up, w_out, sgu_ln_g, sgu_ln_b,
              w_spatial, b_spatial, ln1_g, ln1_b, w_peer_q, peer_sub_keys, peer_u, peer_v,
              ln2_g, ln2_b):
    B, S, D = x.shape
    cs = jax.nn.silu(c)
    for l in range(DEPTH):
        mod = cs @ w_cond[l] + b_cond[l]
        sh1, sc1, gt1, sh2, sc2, gt2 = jnp.split(mod, 6, axis=-1)
        h = _modulate(x, sh1, sc1)
        z = h @ w_in[l]
        q, k, v, gu, gv, ga, gg = jnp.split(z, IN_SPLITS, axis=-1)
        hs = (B, S, N_ATTN_HEADS, ATTN_HEAD_DIM)
        attn = _moba_attention(q.reshape(hs), k.reshape(hs), v.reshape(hs))
        sgu = _chunked_sgu(gu, gv, sgu_ln_g[l], sgu_ln_b[l], w_spatial[l], b_spatial[l])
        merged = (jax.nn.sigmoid(ga) * (attn @ w_attn_up[l])
                  + jax.nn.sigmoid(gg) * (sgu @ w_gmlp_up[l]))
        out = merged @ w_out[l]
        x = _layernorm(ALPHA * x + (1 + gt1[:, None, :]) * out) * ln1_g[l] + ln1_b[l]
        h = _modulate(x, sh2, sc2)
        p = _peer(h, w_peer_q[l], peer_sub_keys[l], peer_u[l], peer_v[l])
        x = _layernorm(ALPHA * x + (1 + gt2[:, None, :]) * p) * ln2_g[l] + ln2_b[l]
    return x


_drawn_inputs = setup_inputs


def setup_inputs(seed=0):
    import zlib

    import numpy as np

    out = dict(_drawn_inputs(seed))
    spreads = {}
    factors = {'sgu_ln_g': 15.884,
     'sgu_ln_b': 17.181,
     'b_spatial': 3.417,
     'ln2_g': 24.55,
     'ln2_b': 23.992}
    for name, (base, spread) in spreads.items():
        noise = np.random.default_rng([zlib.crc32(name.encode()), seed]).standard_normal(out[name].shape)
        drawn = base * np.exp(spread * noise) if base else spread * noise
        out[name] = __import__('jax').numpy.asarray(drawn.astype(out[name].dtype))
    for name, factor in factors.items():
        out[name] = (out[name] * factor).astype(out[name].dtype)
    return out
```

```python
from contextlib import ExitStack

import concourse.bass as bass
from concourse import mybir

F32 = mybir.dt.float32
I32 = mybir.dt.int32
U32 = mybir.dt.uint32
ALU = mybir.AluOpType
ACT = mybir.ActivationFunctionType
AX_X = mybir.AxisListType.X

P = 128
SEQ = 256
D = 1024
TILES = SEQ // P
KC = D // P
HEADS = 8
HD = 64
WIDTH = HEADS * HD
WC = WIDTH // P
BLK = 512
SLOTS = 4
PAIRS = TILES * HEADS
NKEYS = 128
TOPK = 16
GROUP = 8
SHIFT, MASK = 4, TOPK - 1
ALPHA = 2.0 ** 0.25
EPS = 1e-5
LOWEST = -3.0e38
FAR = -1.0e30

STREAM = [("c", 0), ("c", 1), ("c", 2), ("c", 3), ("in", 0), ("c", 4), ("in", 1), ("c", 5), ("in", 2), ("c", 6),
          ("in", 3), ("c", 7), ("in", 4), ("c", 8), ("in", 5), ("c", 9), ("in", 6), ("c", 10), ("in", 7), ("c", 11),
          ("in", 8), ("ua", 0), ("ug", 0), ("o", 0), ("o", 1)]
SLOT = {b: n % SLOTS for n, b in enumerate(STREAM)}
TURN = {b: n // SLOTS for n, b in enumerate(STREAM)}
IN_Q, IN_K, IN_V, IN_GU, IN_GV, IN_GA, IN_GG = 0, 1, 2, 3, 4, 5, 7
PIECES = 18
SH1, SC1, GT1, SH2, SC2, GT2 = range(6)


def build(nc, x, c, w_cond, b_cond, w_in, w_attn_up, w_gmlp_up, w_out, sgu_ln_g, sgu_ln_b,
          w_spatial, b_spatial, ln1_g, ln1_b, w_peer_q, peer_sub_keys, peer_u, peer_v, ln2_g, ln2_b, out):
    with ExitStack() as ctx:
        def sb(name, shape, dt=F32):
            return ctx.enter_context(nc.sbuf_tensor(name, shape, dt))

        def sem(name):
            return ctx.enter_context(nc.semaphore(name))

        x_sb = sb("x_sb", [P, TILES, D])
        h_sb = sb("h_sb", [P, TILES, D])
        hT = sb("hT", [P, KC, SEQ])
        mix = sb("mix", [P, 6 * 1024])
        gates = sb("gates", [P, KC, 2, SEQ])
        cond = sb("cond", [P, 6, D])
        keysT = sb("keysT", [P, 2 * HEADS, NKEYS])
        ring = sb("ring", [P, SLOTS * KC * BLK])
        s_all = sb("s_all", [P, TILES, HEADS, 2 * NKEYS])
        ident = sb("ident", [P, P])
        ones = sb("ones", [P, P])
        zero_tile = sb("zero_tile", [P, P])
        negdist = sb("negdist", [P, 3 * P])
        cacc = sb("cacc", [P, 2, BLK])
        probs = sb("probs", [P, 2, 3 * P])
        probsT = sb("probsT", [P, 2, 3 * P])
        spatT = sb("spatT", [P, HEADS, P])
        sgu_gb = sb("sgu_gb", [P, 2, WIDTH])
        scratch = sb("scratch", [P, 1024])
        brow = sb("brow", [P, HEADS * P])[0:1, :]
        c_col = sb("c_col", [P, 3, KC])
        stats = sb("stats", [P, 8, 2, 6])
        moments = sb("moments", [P, 8, 2])
        std = sb("std", [P, 8, 2])
        gst = sb("gst", [P, 4, 2 * HEADS])
        amax = sb("amax", [P, HEADS, 2])
        asum = sb("asum", [P, 2, HEADS, 2])
        eps = sb("eps", [P, 1])
        iota_i = sb("iota_i", [P, 3 * P + TOPK], I32)
        iota16 = sb("iota16", [P, TOPK])

        m4 = mix[:].rearrange("p (a n) -> p a n", a=6)
        qT = m4[:, 0, :].rearrange("p (c t) -> p c t", c=WC)
        kT = m4[:, 1, :].rearrange("p (c t) -> p c t", c=WC)
        v_sb = m4[:, 2, :].rearrange("p (t n) -> p t n", t=TILES)
        uT = m4[:, 3, :].rearrange("p (c t) -> p c t", c=WC)
        gv_flat = m4[:, 4, :]
        gv = gv_flat.rearrange("p (t n) -> p t n", t=TILES)
        gv_g = gv_flat.rearrange("p (g n) -> p g n", n=HD)
        attnT = m4[:, 5, :].rearrange("p (c t) -> p c t", c=WC)
        keys_nat = s_all[:, 0, :, :].rearrange("p h n -> p (h n)").rearrange("p (m d) -> p m d", d=NKEYS)
        spat_nat = s_all[:, 1, 0:4, :].rearrange("p h n -> p (h n)").rearrange("p (g s) -> p g s", s=P)
        sc = mix[:, 0:256]
        sr = mix[:, 256:512]
        cand = mix[:, 512:768]
        candr = mix[:, 768:1024]
        onehot = mix[:, 1024:1536]
        qTs = mix[:, 1536:2048].rearrange("p (c t) -> p c t", c=2)
        diag = mix[:, 2048:3072].rearrange("p (e n) -> p e n", e=GROUP)
        top = mix[:, 3072:3104]
        topi = mix[:, 3104:3136].bitcast(U32)
        topf = mix[:, 3136:3168]
        best = mix[:, 3168:3184]
        pos = mix[:, 3184:3200].bitcast(U32)
        hilo = mix[:, 3200:3232].bitcast(U32)
        hilof = mix[:, 3232:3264]
        sel = mix[:, 3264:3296]
        nbest = mix[:, 3296:3298]
        esum = mix[:, 3298:3300]
        rsum = mix[:, 3300:3302]
        expv = mix[:, 3302:3334].rearrange("p (a k) -> p a k", a=2)
        acol = mix[:, 3334:3350].rearrange("p (a k) -> p a k", a=2)
        gcol = mix[:, 3350:3366].rearrange("p (a k) -> p a k", a=2)
        wts = mix[:, 3366:3382].rearrange("p (a k) -> p a k", a=2)
        idx = mix[:, 3382:3414].bitcast(U32)
        wpq = gates[:].rearrange("p k a t -> p (k a t)").rearrange("p (s k n) -> p s k n", s=2, k=KC)
        u_ring = ring[:, 0:GROUP * D].rearrange("p (e d) -> p e d", e=GROUP)
        v_ring = ring[:, GROUP * D:2 * GROUP * D].rearrange("p (e d) -> p e d", e=GROUP)

        def slot(b):
            return ring[:, SLOT[b] * KC * BLK:(SLOT[b] + 1) * KC * BLK]

        bank = [ctx.enter_context(nc.psum_tensor(f"bank{i}", [P, BLK], F32)) for i in range(8)]
        PIECE_BANKS = (0, 1)
        SCORE_BANKS = (2, 3)
        TURN_BANK, GATE_BANK, ATTN_BANK, COND_BANK = 4, 5, 6, 7
        OUT_BANKS = ((2, 3), (4, 5))
        HT_BANKS = (0, 1, 6, 7)
        Q_BANKS, S_BANKS = (0, 6), (1, 7)
        ACC_BANKS = ((2, 3), (4, 5))

        x_in = sem("x_in")
        c_in = sem("c_in")
        bcond_in = [sem(f"bcond_in{i}") for i in range(2)]
        keys_in = sem("keys_in")
        spat_in = sem("spat_in")
        sgu_in = sem("sgu_in")
        brow_in = sem("brow_in")
        w_arrived = [sem(f"w_arrived{i}") for i in range(SLOTS)]
        ln1_in = sem("ln1_in")
        ln2_in = sem("ln2_in")
        wpq_in = [sem(f"wpq_in{i}") for i in range(2)]
        u_in = [sem(f"u_in{i}") for i in range(GROUP)]
        v_in = [sem(f"v_in{i}") for i in range(GROUP)]
        out_stored = sem("out_stored")

        consts = sem("consts")
        spat_masked = sem("spat_masked")
        dve_step = sem("dve_step")
        topk_step = sem("topk_step")
        silu_tanh = sem("silu_tanh")
        silu_done = sem("silu_done")
        var_ready = sem("var_ready")
        std_ready = sem("std_ready")
        xn_done = sem("xn_done")
        cacc_ready = sem("cacc_ready")
        cond_sum = sem("cond_sum")
        cond_saved = sem("cond_saved")
        h_ready = sem("h_ready")
        keysT_ready = sem("keysT_ready")
        keysT_saved = sem("keysT_saved")
        spatT_ready = sem("spatT_ready")
        spatT_saved = sem("spatT_saved")
        hT_ready = sem("hT_ready")
        hT_saved_act = sem("hT_saved_act")
        hT_saved_dve = sem("hT_saved_dve")
        piece_ready = sem("piece_ready")
        piece_saved = sem("piece_saved")
        gvar_ready = sem("gvar_ready")
        gstd_ready = sem("gstd_ready")
        vv_ready = sem("vv_ready")
        scores_ready = sem("scores_ready")
        max_ready = sem("max_ready")
        exp_done = sem("exp_done")
        probs_ready = sem("probs_ready")
        turned = sem("turned")
        turned_saved = sem("turned_saved")
        attn_ready = sem("attn_ready")
        attn_saved = sem("attn_saved")
        gate_ready = sem("gate_ready")
        gate_saved = sem("gate_saved")
        up_ready = sem("up_ready")
        merged = sem("merged")
        o_ready = sem("o_ready")
        mod_done = sem("mod_done")
        h2_ready = sem("h2_ready")
        q_ready = sem("q_ready")
        q_saved = sem("q_saved")
        s_ready = sem("s_ready")
        s_saved = sem("s_saved")
        best_ready = sem("best_ready")
        idx_ready = sem("idx_ready")
        wexp_done = sem("wexp_done")
        rsum_ready = sem("rsum_ready")
        dots_done = sem("dots_done")
        gelu_done = sem("gelu_done")
        wts_ready = sem("wts_ready")
        diag_ready = sem("diag_ready")
        v_used = sem("v_used")
        acc_done = sem("acc_done")
        out_ready = sem("out_ready")
        pool_turn = sem("pool_turn")
        dve_turn = sem("dve_turn")

        def hold(engine, turn, s, value):
            engine.wait_ge(s, value)
            engine.sem_inc(turn, 1)

        block = ctx.enter_context(nc.Block())

        @block.sync
        def _(sp):
            w_of = {
                "c": w_cond[0].rearrange("(p k) n -> p k n", k=KC),
                "in": w_in[0].rearrange("(k p) n -> p k n", p=P),
                "o": w_out[0].rearrange("(k p) n -> p k n", p=P),
            }
            up_of = {"ua": w_attn_up[0].rearrange("(k p) n -> p k n", p=P),
                     "ug": w_gmlp_up[0].rearrange("(k p) n -> p k n", p=P)}

            sp.dma_start(x_sb[:], x[0].rearrange("(t p) d -> p t d", p=P)).then_inc(x_in, 16)
            for n, b in enumerate(STREAM):
                kind, i = b
                if n >= SLOTS:
                    old, j = STREAM[n - SLOTS]
                    if old == "c":
                        sp.wait_ge(cacc_ready, j + 1)
                    elif old == "in":
                        sp.wait_ge(piece_ready, 2 * j + 2)
                    else:
                        sp.wait_ge(up_ready, KC)
                if kind in up_of:
                    sp.dma_start(slot(b).rearrange("p (k n) -> p k n", k=WC), up_of[kind]).then_inc(w_arrived[SLOT[b]], 16)
                else:
                    sp.dma_start(slot(b).rearrange("p (k n) -> p k n", k=KC),
                                 w_of[kind][:, :, i * BLK:(i + 1) * BLK]).then_inc(w_arrived[SLOT[b]], 16)
                if b == ("c", 3):
                    sp.dma_start(cond[:, GT1:6, :].rearrange("p a n -> p (a n)"),
                                 b_cond[0:1, 2 * D:6 * D].broadcast_to([P, 4 * D])).then_inc(bcond_in[1], 16)
                if b == ("c", 6):
                    sp.wait_ge(h_ready, TILES)
                    sp.dma_start(cond[:, SH1, :], ln1_g[0:1, :].broadcast_to([P, D])).then_inc(ln1_in, 16)
                    sp.dma_start(cond[:, SC1, :], ln1_b[0:1, :].broadcast_to([P, D])).then_inc(ln1_in, 16)
            wq_of = w_peer_q[0].rearrange("(k p) n -> p k n", p=P)
            sp.wait_ge(merged, KC)
            for a in range(2):
                sp.dma_start(wpq[:, a, :, :], wq_of[:, :, a * 256:(a + 1) * 256]).then_inc(wpq_in[a], 16)
            sp.wait_ge(mod_done, TILES)
            sp.dma_start(cond[:, SH1, :], ln2_g[0:1, :].broadcast_to([P, D])).then_inc(ln2_in, 16)
            sp.dma_start(cond[:, SC1, :], ln2_b[0:1, :].broadcast_to([P, D])).then_inc(ln2_in, 16)
            with sp.Fori(1, HEADS // 2) as i:
                for a in range(2):
                    sp.wait_ge(q_ready, 2 * i - 1 + a)
                    sp.dma_start(wpq[:, a, :, :], wq_of[:, :, bass.ds((2 * i + a) * 256, 256)]).then_inc(wpq_in[a], 16)
            for t in range(TILES):
                sp.wait_ge(out_ready, t + 1)
                sp.dma_start(out[0, t * P:(t + 1) * P, :], h_sb[:, t, :]).then_inc(out_stored, 16)
            sp.wait_ge(out_stored, 16 * TILES)

        @block.gpsimd
        def _(pool):
            nc.gpsimd.memset(ones[:], 1.0).then_inc(consts, 1)
            nc.gpsimd.memset(eps[:], EPS).then_inc(consts, 1)
            nc.gpsimd.memset(ident[:], 0.0).then_inc(consts, 1)
            nc.gpsimd.memset(zero_tile[:], 0.0).then_inc(consts, 1)
            nc.gpsimd.iota(iota_i[:, 0:P], pattern=[[1, P]], base=0, channel_multiplier=-1).then_inc(consts, 1)
            nc.gpsimd.iota(iota_i[:, P:3 * P], pattern=[[1, 2 * P]], base=-P, channel_multiplier=-1).then_inc(consts, 1)
            nc.gpsimd.iota(iota_i[:, 3 * P:3 * P + TOPK], pattern=[[1, TOPK]], base=0, channel_multiplier=0).then_inc(consts, 1)
            pool.wait_ge(consts, 7)
            nc.gpsimd.affine_select(out=ident[:], in_=ident[:], compare_op=ALU.not_equal, fill=1.0, base=0,
                                    pattern=[[-1, P]], channel_multiplier=1).then_inc(consts, 1)
            nc.gpsimd.tensor_copy(negdist[:], iota_i[:, 0:3 * P]).then_inc(consts, 1)
            nc.gpsimd.tensor_copy(iota16[:], iota_i[:, 3 * P:3 * P + TOPK]).then_inc(consts, 1)
            pool.wait_ge(consts, 10)
            nc.gpsimd.affine_select(out=negdist[:, 0:P], in_=negdist[:, 0:P], compare_op=ALU.is_ge, fill=FAR, base=0,
                                    pattern=[[-1, P]], channel_multiplier=1).then_inc(consts, 1)
            nc.gpsimd.affine_select(out=negdist[:, P:3 * P], in_=negdist[:, P:3 * P], compare_op=ALU.is_ge, fill=FAR,
                                    base=P, pattern=[[-1, 2 * P]], channel_multiplier=1).then_inc(consts, 1)
            pool.wait_ge(spat_in, 16)
            nc.gpsimd.affine_select(out=spat_nat, in_=spat_nat, compare_op=ALU.is_ge, fill=0.0, base=0,
                                    pattern=[[0, HEADS], [-1, P]], channel_multiplier=1).then_inc(spat_masked, 1)

            def gather_pair(i, a):
                p = 2 * i + a
                hold(pool, pool_turn, idx_ready, p + 1)
                for g in range(2):
                    for table, rows, used, landed in ((peer_u, u_ring, dots_done, u_in), (peer_v, v_ring, v_used, v_in)):
                        hold(pool, pool_turn, used, (2 * p + g) * GROUP + 1)
                        for e in range(GROUP):
                            k = a * TOPK + g * GROUP + e
                            nc.gpsimd.indirect_dma_start(
                                out=rows[:, e, :], out_offset=None, in_=table[0],
                                in_offset=bass.IndirectOffsetOnAxis(ap=idx[:, k:k + 1], axis=0)).then_inc(landed[e], 16)

            with pool.Fori(0, PAIRS // 2) as i:
                gather_pair(i, 0)
                gather_pair(i, 1)

        @block.scalar
        def _(act):
            act.dma_start(c_col[:, 0, :], c[0].rearrange("(p k) -> p k", k=KC)).then_inc(c_in, 16)
            act.dma_start(cond[:, SH1:GT1, :].rearrange("p a n -> p (a n)"),
                          b_cond[0:1, 0:2 * D].broadcast_to([P, 2 * D])).then_inc(bcond_in[0], 16)
            act.dma_start(spat_nat, w_spatial[0].rearrange("g t s -> t g s")).then_inc(spat_in, 16)
            act.dma_start(brow, b_spatial[0:1].rearrange("a g t -> a (g t)")).then_inc(brow_in, 16)
            act.dma_start(keys_nat, peer_sub_keys[0].rearrange("h c n d -> n (h c) d")).then_inc(keys_in, 16)
            for i, v in enumerate((sgu_ln_g, sgu_ln_b)):
                act.dma_start(sgu_gb[:, i, :], v[0:1].rearrange("a g d -> a (g d)").broadcast_to([P, WIDTH])).then_inc(sgu_in, 16)

            act.wait_ge(c_in, 16)
            nc.scalar.activation(c_col[:, 1, :], c_col[:, 0, :], ACT.Tanh, scale=0.5).then_inc(silu_tanh, 1)

            def root(n):
                act.wait_ge(var_ready, n + 1)
                nc.scalar.activation(std[:, n, 0:1], moments[:, n, 1:2], ACT.Sqrt, bias=eps[:]).then_inc(std_ready, 1)

            act.wait_ge(consts, 2)
            root(0)
            root(1)

            for r in range(2):
                act.wait_ge(spatT_ready, r + 1)
                nc.scalar.activation(spatT[:, 4 * r:4 * r + 4, :].rearrange("p g t -> p (g t)"), bank[r][:],
                                     ACT.Copy).then_inc(spatT_saved, 1)
            for r in range(4):
                act.wait_ge(keysT_ready, r + 1)
                nc.scalar.activation(keysT[:, 4 * r:4 * r + 4, :].rearrange("p g t -> p (g t)"), bank[2 + r][:],
                                     ACT.Copy).then_inc(keysT_saved, 1)

            def save_hT(r, turn):
                act.wait_ge(hT_ready, r + 1 + 4 * turn)
                nc.scalar.activation(hT[:, 2 * r:2 * r + 2, :].rearrange("p k t -> p (k t)"), bank[HT_BANKS[r]][:],
                                     ACT.Copy).then_inc(hT_saved_act, 1)

            save_hT(0, 0)
            save_hT(2, 0)

            def piece(n):
                b, half = n // 2, n % 2
                act.wait_ge(piece_ready, n + 1)
                src = bank[PIECE_BANKS[n % 2]][:]
                two = slice(2 * half, 2 * half + 2)
                if b == IN_Q:
                    ins = nc.scalar.activation(qT[:, two, :].rearrange("p c t -> p (c t)"), src, ACT.Copy, scale=HD ** -0.5)
                elif b == IN_K:
                    ins = nc.scalar.activation(kT[:, two, :].rearrange("p c t -> p (c t)"), src, ACT.Copy)
                elif b == IN_V:
                    ins = nc.scalar.activation(v_sb[:, half, :], src, ACT.Copy)
                elif b == IN_GU:
                    ins = nc.scalar.activation(uT[:, two, :].rearrange("p c t -> p (c t)"), src, ACT.Gelu)
                elif b == IN_GV:
                    ins = nc.scalar.activation(gv[:, half, :], src, ACT.Gelu)
                else:
                    which = int(b >= IN_GG)
                    first = 4 * (b - (IN_GG if which else IN_GA)) + 2 * half
                    ins = nc.scalar.activation(gates[:, first:first + 2, which, :], src.rearrange("p (c t) -> p c t", c=2),
                                               ACT.Tanh, scale=0.5)
                ins.then_inc(piece_saved, 1)

            for n in range(2 * IN_GA):
                piece(n)
            act.wait_ge(gvar_ready, 1)
            nc.scalar.activation(gst[:, 2, :], gst[:, 1, :], ACT.Sqrt, bias=eps[:], scale=1.0 / HD).then_inc(gstd_ready, 1)

            for j in range(HEADS + 2):
                if j < HEADS:
                    for t in range(TILES):
                        act.wait_ge(max_ready, 2 * j + t + 1)
                        cols = slice(0, P) if t == 0 else slice(P, 3 * P)
                        nc.scalar.activation(probs[:, j % 2, cols], probs[:, j % 2, cols], ACT.Exp, bias=amax[:, j, t:t + 1],
                                             accum_out=asum[:, 0, j, t:t + 1]).then_inc(exp_done, 1)
                    piece(2 * IN_GA + j)
                if 1 <= j <= HEADS:
                    act.wait_ge(turned, j)
                    if j >= 3:
                        act.wait_ge(attn_ready, j - 2)
                    nc.scalar.activation(probsT[:, (j - 1) % 2, :], bank[TURN_BANK][:, 0:3 * P], ACT.Copy).then_inc(turned_saved, 1)
                if j >= 3 and j % 2 == 1:
                    m = (j - 3) // 2
                    act.wait_ge(attn_ready, 2 * m + 2)
                    nc.scalar.activation(attnT[:, m, :], bank[ATTN_BANK][:, (m % 2) * SEQ:(m % 2 + 1) * SEQ],
                                         ACT.Copy).then_inc(attn_saved, 1)

            for t in range(TILES):
                root(2 + 2 * t)
                root(3 + 2 * t)
            save_hT(0, 1)
            save_hT(2, 1)

            def save_q(h, a):
                act.wait_ge(q_ready, h + 1)
                nc.scalar.activation(qTs.rearrange("p c t -> p (c t)"), bank[Q_BANKS[a]][:], ACT.Copy).then_inc(q_saved, 1)
                act.wait_ge(s_ready, h + 1)
                nc.scalar.activation(s_all[:, :, bass.ds(h, 1), :].rearrange("p t h n -> p t (h n)"),
                                     bank[S_BANKS[a]][:].rearrange("p (t n) -> p t n", t=TILES),
                                     ACT.Copy).then_inc(s_saved, 1)

            def softmax_exp(p, a):
                act.wait_ge(best_ready, p + 1)
                nc.scalar.activation(expv[:, a, :], best, ACT.Exp, bias=nbest[:, a:a + 1],
                                     accum_out=esum[:, a:a + 1]).then_inc(wexp_done, 1)

            def weigh(i, a, head=None, following=True):
                p = 2 * i + a
                if head is not None:
                    save_q(head, 1 - a)
                for g in range(2):
                    n = 2 * p + g
                    act.wait_ge(dots_done, GROUP * n + GROUP + 1)
                    nc.scalar.activation(gcol[:, g, :], acol[:, g, :], ACT.Gelu).then_inc(gelu_done, 1)
                    if g == 1 and following:
                        softmax_exp(p + 1, 1 - a)
                    act.wait_ge(wts_ready, n + 1)
                    act.wait_ge(v_used, GROUP * n + 1)
                    for e in range(GROUP):
                        nc.scalar.activation(diag[:, e, :], ident[:], ACT.Copy, scale=wts[:, g, e:e + 1]).then_inc(diag_ready, 1)

            save_q(0, 0)
            softmax_exp(0, 0)
            with act.Fori(0, HEADS // 2 - 1) as i:
                weigh(i, 0, head=2 * i + 1)
                weigh(i, 1, head=2 * i + 2)
            weigh(HEADS // 2 - 1, 0, head=HEADS - 1)
            weigh(HEADS // 2 - 1, 1)
            with act.Fori(HEADS // 2, PAIRS // 2 - 1) as i:
                weigh(i, 0)
                weigh(i, 1)
            root(6)
            weigh(PAIRS // 2 - 1, 0)
            weigh(PAIRS // 2 - 1, 1, following=False)
            root(7)

        @block.vector
        def _(dve):
            steps = [0]

            def link(ins):
                steps[0] += 1
                ins.then_inc(dve_step, 1)
                dve.wait_ge(dve_step, steps[0])

            V = nc.vector

            def variance(n, src):
                for i in range(2):
                    last = V.bn_stats(stats[:, n, i, :], src[:, i * BLK:(i + 1) * BLK])
                    if i == 0:
                        last.then_inc(dve_step, 1)
                        steps[0] += 1
                link(last)
                V.bn_aggr(moments[:, n, :], stats[:, n, :, :].rearrange("p a b -> p (a b)")).then_inc(var_ready, 1)

            def normalise(n, dst, src):
                dve.wait_ge(std_ready, n + 1)
                link(V.reciprocal(std[:, n, 1:2], std[:, n, 0:1]))
                return V.tensor_scalar(dst, src, moments[:, n, 0:1], std[:, n, 1:2], ALU.subtract, ALU.mult)

            dve.wait_ge(x_in, 16)
            for t in range(TILES):
                variance(t, x_sb[:, t, :])
            dve.wait_ge(silu_tanh, 1)
            link(V.scalar_tensor_tensor(out=c_col[:, 2, :], in0=c_col[:, 1, :], scalar=1.0, in1=c_col[:, 0, :],
                                        op0=ALU.add, op1=ALU.mult))
            link(V.tensor_scalar(c_col[:, 2, :], c_col[:, 2, :], 0.5, None, ALU.mult))
            for t in range(TILES):
                link(normalise(t, h_sb[:, t, :], x_sb[:, t, :]))

            def cond_block(n):
                b = ("c", n)
                dve.wait_ge(w_arrived[SLOT[b]], 16 * (TURN[b] + 1))
                if n >= 2:
                    dve.wait_ge(cond_sum, n - 1)
                w = slot(b).rearrange("p (k n) -> p k n", k=KC)
                acc = cacc[:, n % 2, :]
                link(V.tensor_scalar(acc, w[:, 0, :], c_col[:, 2, 0:1], None, ALU.mult))
                for k in range(1, KC):
                    ins = V.scalar_tensor_tensor(out=acc, in0=w[:, k, :], scalar=c_col[:, 2, k:k + 1], in1=acc,
                                                 op0=ALU.mult, op1=ALU.add)
                    if k < KC - 1:
                        link(ins)
                ins.then_inc(cacc_ready, 1)

            def cond_save(n):
                dve.wait_ge(cond_sum, n + 1)
                part = cond[:, n // 2, (n % 2) * BLK:(n % 2 + 1) * BLK]
                one = 0.0 if n // 2 in (SH1, SH2) else 1.0
                V.scalar_tensor_tensor(out=part, in0=bank[COND_BANK][:], scalar=one, in1=part,
                                       op0=ALU.add, op1=ALU.add).then_inc(cond_saved, 1)

            dve.wait_ge(bcond_in[0], 16)
            for n in range(4):
                cond_block(n)
                if n:
                    cond_save(n - 1)
            cond_save(3)
            dve.wait_ge(cond_saved, 4)
            for t in range(TILES):
                link(V.tensor_tensor(h_sb[:, t, :], h_sb[:, t, :], cond[:, SC1, :], ALU.mult))
                V.tensor_tensor(h_sb[:, t, :], h_sb[:, t, :], cond[:, SH1, :], ALU.add).then_inc(h_ready, 1)

            def save_hT(r, turn):
                dve.wait_ge(hT_ready, r + 1 + 4 * turn)
                V.tensor_copy(hT[:, 2 * r:2 * r + 2, :].rearrange("p k t -> p (k t)"),
                              bank[HT_BANKS[r]][:]).then_inc(hT_saved_dve, 1)

            save_hT(1, 0)
            save_hT(3, 0)

            dve.wait_ge(bcond_in[1], 16)
            for n in range(4, 9):
                cond_block(n)
                if n > 4:
                    cond_save(n - 1)
            cond_save(8)

            def wide(v):
                return v.unsqueeze(2).broadcast_to([P, 2 * HEADS, HD])

            sq = scratch[:].rearrange("p (g n) -> p g n", n=HD)
            dve.wait_ge(piece_saved, 2 * IN_GV + 2)
            link(V.tensor_reduce(gst[:, 0, :], gv_g, AX_X, ALU.add))
            link(V.tensor_scalar(gst[:, 0, :], gst[:, 0, :], 1.0 / HD, None, ALU.mult))
            link(V.tensor_tensor(gv_g, gv_g, wide(gst[:, 0, :]), ALU.subtract))
            link(V.tensor_tensor(sq, gv_g, gv_g, ALU.mult))
            V.tensor_reduce(gst[:, 1, :], sq, AX_X, ALU.add).then_inc(gvar_ready, 1)
            dve.wait_ge(gstd_ready, 1)
            link(V.reciprocal(gst[:, 3, :], gst[:, 2, :]))
            link(V.tensor_tensor(gv_g, gv_g, wide(gst[:, 3, :]), ALU.mult))
            dve.wait_ge(sgu_in, 32)
            for i, op in ((0, ALU.mult), (1, ALU.add)):
                ins = V.tensor_tensor(gv, gv, sgu_gb[:, i, :].unsqueeze(1).broadcast_to([P, TILES, WIDTH]), op)
                if i == 0:
                    link(ins)
            ins.then_inc(vv_ready, 1)

            def save_gate(r):
                dve.wait_ge(gate_ready, r + 1)
                part = uT[:, 2 * r:2 * r + 2, :].rearrange("p c t -> p (c t)")
                V.tensor_tensor(part, part, bank[GATE_BANK][:], ALU.mult).then_inc(gate_saved, 1)

            dve.wait_ge(consts, 12)
            for j in range(HEADS):
                pj = probs[:, j % 2, :]
                if j >= 2:
                    dve.wait_ge(turned, j - 1)
                dve.wait_ge(scores_ready, j + 1)
                link(V.scalar_tensor_tensor(out=pj, in0=negdist[:], scalar=2.0 ** -(j + 1), in1=bank[SCORE_BANKS[j % 2]][:, 0:3 * P],
                                            op0=ALU.mult, op1=ALU.add))
                for t in range(TILES):
                    cols = slice(0, P) if t == 0 else slice(P, 3 * P)
                    V.tensor_reduce(amax[:, j, t:t + 1], pj[:, cols], AX_X, ALU.max, negate=True).then_inc(max_ready, 1)
                dve.wait_ge(exp_done, 2 * j + 2)
                link(V.reciprocal(asum[:, 1, j, :], asum[:, 0, j, :]))
                for t in range(TILES):
                    cols = slice(0, P) if t == 0 else slice(P, 3 * P)
                    V.tensor_scalar(pj[:, cols], pj[:, cols], asum[:, 1, j, t:t + 1], None, ALU.mult).then_inc(probs_ready, 1)
                if j in (0, 2, 4):
                    cond_block(9 + j // 2)
                if j in (1, 3, 5):
                    cond_save(9 + j // 2)
                if j == 5:
                    save_gate(0)
            save_gate(1)

            tmp = scratch[:, 0:2 * SEQ]
            dve.wait_ge(piece_saved, PIECES)
            for n in range(KC):
                dve.wait_ge(up_ready, n + 1)
                if n:
                    dve.wait_ge(merged, n)
                link(V.scalar_tensor_tensor(out=tmp, in0=gates[:, n, :, :].rearrange("p a t -> p (a t)"), scalar=1.0,
                                            in1=bank[PIECE_BANKS[n % 2]][:], op0=ALU.add, op1=ALU.mult))
                V.tensor_tensor(hT[:, n, :], tmp[:, 0:SEQ], tmp[:, SEQ:2 * SEQ], ALU.add).then_inc(merged, 1)

            def residual(t, banks, gate, halve, dst):
                for i in range(2):
                    cols = slice(i * BLK, (i + 1) * BLK)
                    ins = V.scalar_tensor_tensor(out=dst[:, cols], in0=bank[banks[i]][:], scalar=halve,
                                                 in1=cond[:, gate, cols], op0=ALU.mult, op1=ALU.mult)
                    ins.then_inc(dve_step, 1)
                    steps[0] += 1
                dve.wait_ge(dve_step, steps[0])
                link(V.scalar_tensor_tensor(out=dst, in0=x_sb[:, t, :], scalar=ALPHA, in1=dst, op0=ALU.mult, op1=ALU.add))

            dve.wait_ge(ln1_in, 32)
            dve.wait_ge(cond_saved, 12)
            for t in range(TILES):
                ht, xt = h_sb[:, t, :], x_sb[:, t, :]
                dve.wait_ge(o_ready, t + 1)
                residual(t, OUT_BANKS[t], GT1, 0.5, ht)
                variance(2 + 2 * t, ht)
                link(normalise(2 + 2 * t, xt, ht))
                link(V.tensor_tensor(xt, xt, cond[:, SH1, :], ALU.mult))
                V.tensor_tensor(xt, xt, cond[:, SC1, :], ALU.add).then_inc(mod_done, 1)
                dve.wait_ge(mod_done, t + 1)
                variance(3 + 2 * t, xt)
                link(normalise(3 + 2 * t, ht, xt))
                link(V.tensor_tensor(ht, ht, cond[:, SC2, :], ALU.mult))
                V.tensor_tensor(ht, ht, cond[:, SH2, :], ALU.add).then_inc(h2_ready, 1)
            save_hT(1, 1)
            save_hT(3, 1)

            TOPK_STEPS = 24

            def topk(p, a, need):
                n = [0]

                def step(*many):
                    for ins in many:
                        n[0] += 1
                        ins.then_inc(topk_step, 1)
                    hold(dve, dve_turn, topk_step, p * TOPK_STEPS + n[0])

                hold(dve, dve_turn, s_saved, need)
                step(V.tensor_copy(sc, s_all[:].rearrange("p t h n -> p (t h n)")[:, bass.ds(p * 256, 256)]))
                half = [slice(0, NKEYS), slice(NKEYS, 2 * NKEYS)]
                hi8 = [slice(0, 8), slice(TOPK, TOPK + 8)]
                lo8 = [slice(8, TOPK), slice(TOPK + 8, 2 * TOPK)]
                step(*[V.max(top[:, hi8[c]], sc[:, half[c]]) for c in range(2)])
                step(*[V.match_replace(sr[:, half[c]], top[:, hi8[c]], sc[:, half[c]], LOWEST) for c in range(2)],
                     *[V.max_index(topi[:, hi8[c]], top[:, hi8[c]], sc[:, half[c]]) for c in range(2)])
                step(*[V.max(top[:, lo8[c]], sr[:, half[c]]) for c in range(2)])
                step(*[V.max_index(topi[:, lo8[c]], top[:, lo8[c]], sr[:, half[c]]) for c in range(2)],
                     V.tensor_tensor(cand.rearrange("p (i j) -> p i j", i=TOPK),
                                     top[:, 0:TOPK].unsqueeze(2).broadcast_to([P, TOPK, TOPK]),
                                     top[:, TOPK:2 * TOPK].unsqueeze(1).broadcast_to([P, TOPK, TOPK]), ALU.add))
                step(V.max(best[:, 0:8], cand))
                step(V.match_replace(candr, best[:, 0:8], cand, LOWEST),
                     V.max_index(pos[:, 0:8], best[:, 0:8], cand),
                     V.tensor_scalar(nbest[:, a:a + 1], best[:, 0:1], -1.0, None, ALU.mult))
                V.max(best[:, 8:TOPK], candr).then_inc(best_ready, 1)
                hold(dve, dve_turn, best_ready, p + 1)
                step(V.max_index(pos[:, 8:TOPK], best[:, 8:TOPK], candr),
                     V.tensor_copy(topf, topi))
                step(V.tensor_scalar(hilo[:, 0:TOPK], pos, SHIFT, None, ALU.logical_shift_right),
                     V.tensor_scalar(hilo[:, TOPK:2 * TOPK], pos, MASK, None, ALU.bitwise_and))
                step(V.tensor_copy(hilof, hilo))
                oh = onehot.rearrange("p (m i) -> p m i", i=TOPK)
                oh4 = onehot.rearrange("p (c k i) -> p c k i", c=2, k=TOPK)
                step(V.tensor_tensor(oh, hilof.unsqueeze(2).broadcast_to([P, 2 * TOPK, TOPK]),
                                     iota16[:].unsqueeze(1).broadcast_to([P, 2 * TOPK, TOPK]), ALU.is_equal))
                step(V.tensor_tensor(oh4, oh4, topf.rearrange("p (c i) -> p c i", c=2).unsqueeze(2)
                                     .broadcast_to([P, 2, TOPK, TOPK]), ALU.mult))
                step(V.tensor_reduce(sel, oh, AX_X, ALU.add))
                assert n[0] == TOPK_STEPS, n[0]
                hold(dve, dve_turn, v_used, p * TOPK - TOPK + 1 if not isinstance(p, int) or p else 1)
                V.scalar_tensor_tensor(out=idx[:, a * TOPK:(a + 1) * TOPK], in0=sel[:, 0:TOPK], scalar=float(NKEYS),
                                       in1=sel[:, TOPK:2 * TOPK], op0=ALU.mult, op1=ALU.add).then_inc(idx_ready, 1)

            def weights(p, a, g):
                if g == 0:
                    dve.wait_ge(wexp_done, p + 1)
                    V.reciprocal(rsum[:, a:a + 1], esum[:, a:a + 1]).then_inc(rsum_ready, 1)
                dve.wait_ge(rsum_ready, p + 1)
                dve.wait_ge(gelu_done, 2 * p + g + 1)
                V.scalar_tensor_tensor(out=wts[:, g, :], in0=gcol[:, g, :], scalar=rsum[:, a:a + 1],
                                       in1=expv[:, a, g * GROUP:(g + 1) * GROUP], op0=ALU.mult, op1=ALU.mult).then_inc(wts_ready, 1)

            def dots(i, a, t, need=None, following=True):
                p = 2 * i + a
                for g in range(2):
                    for e in range(GROUP):
                        if g == 1 and e == 2:
                            weights(p, a, 0)
                        dve.wait_ge(u_in[e], 16 * (2 * p + g + 1))
                        V.tensor_tensor_reduce(u_ring[:, e, :], u_ring[:, e, :], h_sb[:, t, :], 1.0, 0.0, ALU.mult, ALU.add,
                                               acol[:, g, e:e + 1]).then_inc(dots_done, 1)
                if following:
                    topk(p + 1, 1 - a, need if need is not None else p + 2)
                weights(p, a, 1)

            def finish(t):
                ht = h_sb[:, t, :]
                dve.wait_ge(ln2_in, 32)
                dve.wait_ge(acc_done, t + 1)
                residual(t, ACC_BANKS[t], GT2, 1.0, ht)
                variance(6 + t, ht)
                link(normalise(6 + t, ht, ht))
                link(V.tensor_tensor(ht, ht, cond[:, SH1, :], ALU.mult))
                V.tensor_tensor(ht, ht, cond[:, SC1, :], ALU.add).then_inc(out_ready, 1)

            dve.wait_ge(v_used, 1)
            dve.sem_inc(dots_done, 1)
            topk(0, 0, 1)
            with dve.Fori(0, HEADS // 2 - 1) as i:
                dots(i, 0, 0)
                dots(i, 1, 0)
            dots(HEADS // 2 - 1, 0, 0)
            dots(HEADS // 2 - 1, 1, 0, need=HEADS)
            with dve.Fori(HEADS // 2, PAIRS // 2 - 1) as i:
                dots(i, 0, 1, need=HEADS)
                dots(i, 1, 1, need=HEADS)
            finish(0)
            dots(PAIRS // 2 - 1, 0, 1, need=HEADS)
            dots(PAIRS // 2 - 1, 1, 1, following=False)
            finish(1)

        @block.tensor
        def _(pe):
            T = nc.tensor
            pe.wait_ge(consts, 8)

            pe.wait_ge(spat_masked, 1)
            for r in range(2):
                for g in range(4):
                    last = T.transpose(bank[r][:, g * P:(g + 1) * P], spat_nat[:, 4 * r + g, :], ident[:])
                last.then_inc(spatT_ready, 1)
            pe.wait_ge(keys_in, 16)
            for r in range(4):
                for g in range(4):
                    last = T.transpose(bank[2 + r][:, g * P:(g + 1) * P], keys_nat[:, 4 * r + g, :], ident[:])
                last.then_inc(keysT_ready, 1)

            def cond_total(n):
                pe.wait_ge(cacc_ready, n + 1)
                if n:
                    pe.wait_ge(cond_saved, n)
                T.matmul(bank[COND_BANK][:], ones[:], cacc[:, n % 2, :], start=True, stop=True).then_inc(cond_sum, 1)

            for n in range(4):
                cond_total(n)

            def transpose_h(ready):
                for t in range(TILES):
                    pe.wait_ge(ready, t + 1)
                    for r in range(4):
                        for k in range(2):
                            ch = 2 * r + k
                            last = T.transpose(bank[HT_BANKS[r]][:, k * SEQ + t * P:k * SEQ + (t + 1) * P],
                                               h_sb[:, t, ch * P:(ch + 1) * P], ident[:])
                        if t == TILES - 1:
                            last.then_inc(hT_ready, 1)

            pe.wait_ge(spatT_saved, 2)
            pe.wait_ge(cond_saved, 4)
            transpose_h(h_ready)

            def arrived(b):
                pe.wait_ge(w_arrived[SLOT[b]], 16 * (TURN[b] + 1))

            def piece(n):
                b, half = n // 2, n % 2
                w = slot(("in", b)).rearrange("p (k n) -> p k n", k=KC)
                if half == 0:
                    arrived(("in", b))
                if n >= 2:
                    pe.wait_ge(piece_saved, n - 1)
                dst = bank[PIECE_BANKS[n % 2]]
                if b in (IN_V, IN_GV):
                    for k in range(KC):
                        last = T.matmul(dst[:], hT[:, k, half * P:(half + 1) * P], w[:, k, :], start=(k == 0), stop=(k == KC - 1))
                else:
                    for m in range(2):
                        col = (2 * half + m) * P
                        for k in range(KC):
                            last = T.matmul(dst[:, m * SEQ:(m + 1) * SEQ], w[:, k, col:col + P], hT[:, k, :],
                                            start=(k == 0), stop=(k == KC - 1))
                last.then_inc(piece_ready, 1)

            pe.wait_ge(hT_saved_act, 2)
            pe.wait_ge(hT_saved_dve, 2)
            for b in range(IN_GA):
                piece(2 * b)
                piece(2 * b + 1)
                cond_total(4 + b)

            def scores(j):
                rows = slice(HD * (j % 2), HD * (j % 2) + HD)
                if j == 0:
                    pe.wait_ge(keysT_saved, 4)
                if j >= 2:
                    pe.wait_ge(max_ready, 2 * j - 2)
                dst = bank[SCORE_BANKS[j % 2]]
                T.matmul(dst[:, 0:P], qT[rows, j // 2, 0:P], kT[rows, j // 2, 0:P], start=True, stop=True)
                T.matmul(dst[:, P:3 * P], qT[rows, j // 2, P:SEQ], kT[rows, j // 2, :], start=True, stop=True).then_inc(scores_ready, 1)

            def turn(j):
                pe.wait_ge(probs_ready, 2 * j + 2)
                if j:
                    pe.wait_ge(turned_saved, j)
                for m in range(3):
                    last = T.transpose(bank[TURN_BANK][:, m * P:(m + 1) * P], probs[:, j % 2, m * P:(m + 1) * P], ident[:])
                last.then_inc(turned, 1)

            def attend(j):
                pe.wait_ge(turned_saved, j + 1)
                if j % 2 == 0 and j >= 2:
                    pe.wait_ge(attn_saved, j // 2)
                rows = slice(HD * (j % 2), HD * (j % 2) + HD)
                col = (j // 2 % 2) * SEQ
                dst = bank[ATTN_BANK]
                vh = [v_sb[:, t, j * HD:(j + 1) * HD] for t in range(TILES)]
                pt = probsT[:, j % 2, :]
                T.matmul(dst[rows, col:col + P], vh[0], pt[:, 0:P], start=True, stop=True)
                T.matmul(dst[rows, col + P:col + SEQ], vh[0], pt[:, P:2 * P], start=True, stop=False)
                T.matmul(dst[rows, col + P:col + SEQ], vh[1], pt[:, 2 * P:3 * P], start=False, stop=True).then_inc(attn_ready, 1)

            def spatial(r):
                if r == 0:
                    pe.wait_ge(vv_ready, 1)
                    pe.wait_ge(brow_in, 16)
                else:
                    pe.wait_ge(gate_saved, r)
                for g in range(4 * r, 4 * r + 4):
                    rows = slice(HD * (g % 2), HD * (g % 2) + HD)
                    for t in range(TILES):
                        col = (g // 2 % 2) * SEQ + t * P
                        dst = bank[GATE_BANK][rows, col:col + P]
                        T.matmul(dst, gv[:, t, g * HD:(g + 1) * HD], spatT[:, g, :], start=True, stop=False)
                        last = T.matmul(dst, ones[0:1, 0:HD], brow[:, g * P:(g + 1) * P], start=False, stop=True)
                last.then_inc(gate_ready, 1)

            for j in range(HEADS + 2):
                if j < HEADS:
                    scores(j)
                    piece(2 * IN_GA + j)
                if 1 <= j <= HEADS:
                    turn(j - 1)
                if j >= 2:
                    attend(j - 2)
                if j in (1, 3, 5):
                    cond_total(9 + j // 2)
                if j in (4, 6):
                    spatial(j // 2 - 2)

            arrived(("ua", 0))
            arrived(("ug", 0))
            pe.wait_ge(gate_saved, 2)
            pe.wait_ge(attn_saved, WC)
            pe.wait_ge(piece_saved, PIECES)
            ups = [(slot((kind, 0)).rearrange("p (k n) -> p k n", k=WC), src) for kind, src in (("ua", attnT), ("ug", uT))]
            for n in range(KC):
                if n >= 2:
                    pe.wait_ge(merged, n - 1)
                for m, (w, src) in enumerate(ups):
                    for k in range(WC):
                        last = T.matmul(bank[PIECE_BANKS[n % 2]][:, m * SEQ:(m + 1) * SEQ], w[:, k, n * P:(n + 1) * P],
                                        src[:, k, :], start=(k == 0), stop=(k == WC - 1))
                last.then_inc(up_ready, 1)

            arrived(("o", 0))
            arrived(("o", 1))
            pe.wait_ge(merged, KC)
            for t in range(TILES):
                for m in range(2):
                    w = slot(("o", m)).rearrange("p (k n) -> p k n", k=KC)
                    for k in range(KC):
                        last = T.matmul(bank[OUT_BANKS[t][m]][:], hT[:, k, t * P:(t + 1) * P], w[:, k, :],
                                        start=(k == 0), stop=(k == KC - 1))
                last.then_inc(o_ready, 1)

            pe.wait_ge(cond_saved, 12)
            transpose_h(h2_ready)
            pe.wait_ge(hT_saved_act, 4)
            pe.wait_ge(hT_saved_dve, 4)

            def retrieve(h, a, first=False):
                pe.wait_ge(wpq_in[a], 16 * ((h - a) // 2 + 1) if isinstance(h, int) else 8 * (h - a) + 16)
                if first is False:
                    pe.wait_ge(s_saved, h)
                for m in range(2):
                    for k in range(KC):
                        last = T.matmul(bank[Q_BANKS[a]][:, m * SEQ:(m + 1) * SEQ], wpq[:, a, k, m * P:(m + 1) * P], hT[:, k, :],
                                        start=(k == 0), stop=(k == KC - 1))
                last.then_inc(q_ready, 1)
                pe.wait_ge(q_saved, h + 1)
                for t in range(TILES):
                    for m in range(2):
                        last = T.matmul(bank[S_BANKS[a]][:, (2 * t + m) * P:(2 * t + m + 1) * P], qTs[:, m, t * P:(t + 1) * P],
                                        keysT[:].rearrange("p m n -> p (m n)")[:, bass.ds((2 * h + m) * NKEYS, NKEYS)],
                                        start=True, stop=True)
                last.then_inc(s_ready, 1)

            def clear(t):
                for m in range(2):
                    last = T.matmul(bank[ACC_BANKS[t][m]][:, 0:BLK], zeros, h_sb[:, t, m * BLK:(m + 1) * BLK], start=True,
                                    stop=False, skip_group_check=True)
                return last

            def add_rows(i, a, t, head=None):
                if head is not None:
                    retrieve(head, 1 - a)
                for g in range(2):
                    n = 2 * (2 * i + a) + g
                    for e in range(GROUP):
                        pe.wait_ge(v_in[e], 16 * (n + 1))
                        pe.wait_ge(diag_ready, GROUP * n + e + 1)
                        for m in range(2):
                            last = T.matmul(bank[ACC_BANKS[t][m]][:], diag[:, e, :], v_ring[:, e, m * BLK:(m + 1) * BLK],
                                            start=False, stop=False, skip_group_check=True)
                        last.then_inc(v_used, 1)

            def close(t):
                for m in range(2):
                    last = T.matmul(bank[ACC_BANKS[t][m]][:], zeros, h_sb[:, t, m * BLK:(m + 1) * BLK], start=False,
                                    stop=True, skip_group_check=True)
                last.then_inc(acc_done, 1)

            zeros = zero_tile[:]
            clear(0)
            clear(1).then_inc(v_used, 1)
            retrieve(0, 0, first=True)
            with pe.Fori(0, HEADS // 2 - 1) as i:
                add_rows(i, 0, 0, head=2 * i + 1)
                add_rows(i, 1, 0, head=2 * i + 2)
            add_rows(HEADS // 2 - 1, 0, 0, head=HEADS - 1)
            add_rows(HEADS // 2 - 1, 1, 0)
            close(0)
            with pe.Fori(HEADS // 2, PAIRS // 2) as i:
                add_rows(i, 0, 1)
                add_rows(i, 1, 1)
            close(1)


_INS = ['x', 'c', 'w_cond', 'b_cond', 'w_in', 'w_attn_up', 'w_gmlp_up', 'w_out', 'sgu_ln_g', 'sgu_ln_b',
        'w_spatial', 'b_spatial', 'ln1_g', 'ln1_b', 'w_peer_q', 'peer_sub_keys', 'peer_u', 'peer_v', 'ln2_g', 'ln2_b']


def kernel(**inputs):
    import numpy as _np
    import concourse.bacc as _bacc
    from concourse import mybir as _mybir
    from concourse.bass_utils import run_bass_kernel_spmd as _run

    nc = _bacc.Bacc("TRN2", target_bir_lowering=False, num_devices=1)
    arrays, args = {}, []
    for name in _INS:
        a = _np.ascontiguousarray(inputs[name])
        arrays[f"in_{name}_dram"] = a
        args.append(nc.dram_tensor(f"in_{name}_dram", a.shape, _mybir.dt.from_np(a.dtype), kind="ExternalInput").ap())
    out = nc.dram_tensor("out_0_dram", (1, SEQ, D), F32, kind="ExternalOutput").ap()
    build(nc, *args, out)
    r = _run(nc, [arrays], core_ids=[0])
    return r.results[0]["out_0_dram"]
```

```python
from contextlib import ExitStack

import concourse.bass as bass
from concourse import mybir

F32 = mybir.dt.float32
I32 = mybir.dt.int32
U32 = mybir.dt.uint32
ALU = mybir.AluOpType
ACT = mybir.ActivationFunctionType
AX_X = mybir.AxisListType.X

P = 128
SEQ = 256
D = 1024
TILES = SEQ // P
KC = D // P
HEADS = 8
HD = 64
WIDTH = HEADS * HD
WC = WIDTH // P
BLK = 512
SLOTS = 4
PAIRS = TILES * HEADS
NKEYS = 128
TOPK = 16
GROUP = 8
SHIFT, MASK = 4, TOPK - 1
ALPHA = 2.0 ** 0.25
EPS = 1e-5
LOWEST = -3.0e38
FAR = -1.0e30

STREAM = [("c", 0), ("c", 1), ("c", 2), ("c", 3), ("in", 0), ("c", 4), ("in", 1), ("c", 5), ("in", 2), ("c", 6),
          ("in", 3), ("c", 7), ("in", 4), ("c", 8), ("in", 5), ("c", 9), ("in", 6), ("c", 10), ("in", 7), ("c", 11),
          ("in", 8), ("ua", 0), ("ug", 0), ("o", 0), ("o", 1)]
SLOT = {b: n % SLOTS for n, b in enumerate(STREAM)}
TURN = {b: n // SLOTS for n, b in enumerate(STREAM)}
IN_Q, IN_K, IN_V, IN_GU, IN_GV, IN_GA, IN_GG = 0, 1, 2, 3, 4, 5, 7
PIECES = 18
GT1, SH2, SC2, GT2 = range(4)
LN_G, LN_B = 0, 1
UROW, VROW, ROWS = 4, 12, 16


def build(nc, x, c, w_cond, b_cond, w_in, w_attn_up, w_gmlp_up, w_out, sgu_ln_g, sgu_ln_b,
          w_spatial, b_spatial, ln1_g, ln1_b, w_peer_q, peer_sub_keys, peer_u, peer_v, ln2_g, ln2_b, out):
    with ExitStack() as ctx:
        def sb(name, shape, dt=F32):
            return ctx.enter_context(nc.sbuf_tensor(name, shape, dt))

        def sem(name):
            return ctx.enter_context(nc.semaphore(name))

        x_sb = sb("x_sb", [P, TILES, D])
        h_sb = sb("h_sb", [P, TILES, D])
        hT = sb("hT", [P, KC, SEQ])
        wpq = sb("wpq", [P, HEADS * KC * 256])
        small = sb("small", [P, 3 * 1024])
        cond = sb("cond", [P, 4, D])
        ln1 = sb("ln1", [P, 2, D])
        ln2 = sb("ln2", [P, 2, D])
        keysT = sb("keysT", [P, 2 * HEADS, NKEYS])
        ring = sb("ring", [P, ROWS * D])
        ident = sb("ident", [P, P])
        ones = sb("ones", [P, P])
        zero_tile = sb("zero_tile", [P, P])
        c_col = sb("c_col", [P, 3, KC])
        mod1 = sb("mod1", [P, 2, KC])
        stats = sb("stats", [P, 8, 2, 6])
        moments = sb("moments", [P, 8, 2])
        std = sb("std", [P, 8, 2])
        gst = sb("gst", [P, 4, 2 * HEADS])
        amax = sb("amax", [P, HEADS, 2])
        asum = sb("asum", [P, 2, HEADS, 2])
        eps = sb("eps", [P, 1])
        iota16 = sb("iota16", [P, TOPK])

        qT = wpq[:, 0:1024].rearrange("p (c t) -> p c t", c=WC)
        kT = wpq[:, 1024:2048].rearrange("p (c t) -> p c t", c=WC)
        v_sb = wpq[:, 2048:3072].rearrange("p (t n) -> p t n", t=TILES)
        negdist = wpq[:, 3072:3456]
        probs = wpq[:, 3456:4224].rearrange("p (a n) -> p a n", a=2)
        probsT = wpq[:, 4224:4992].rearrange("p (a n) -> p a n", a=2)
        spatT = wpq[:, 4992:6016].rearrange("p (g t) -> p g t", t=P)
        sgu_gb = wpq[:, 6016:7040].rearrange("p (a n) -> p a n", a=2)
        brow = wpq[0:1, 7040:8064]
        iota_i = wpq[:, 8064:8464].bitcast(I32)
        EARLY = 4
        cacc = wpq[:, 8464:9488].rearrange("p (a n) -> p a n", a=2)
        scratch = wpq[:, 9488:10512]
        gates = wpq[:, 12288:16384]
        gates_v = gates.rearrange("p (t k a n) -> p t k a n", t=TILES, k=KC, a=2)
        b1_row = wpq[0:1, 0:2 * D]
        keys_nat = wpq[:, 12288:14336].rearrange("p (m d) -> p m d", d=NKEYS)
        uT = small[:, 0:1024].rearrange("p (c t) -> p c t", c=WC)
        gv_flat = small[:, 1024:2048]
        gv = gv_flat.rearrange("p (t n) -> p t n", t=TILES)
        gv_g = gv_flat.rearrange("p (g n) -> p g n", n=HD)
        attnT = small[:, 2048:3072].rearrange("p (c t) -> p c t", c=WC)
        spat_nat = small[:, 2048:3072].rearrange("p (g s) -> p g s", s=P)
        sc = small[:, 0:256]
        sr = small[:, 256:512]
        cand = small[:, 512:768]
        candr = small[:, 768:1024]
        onehot = small[:, 512:1024]
        q_tok = small[:, 1024:1280]
        qTs = small[:, 1280:1536].rearrange("p (c t) -> p c t", c=2)
        diag = small[:, 1536:2560].rearrange("p (e n) -> p e n", e=GROUP)
        top = small[:, 2560:2592]
        topi = small[:, 2592:2624].bitcast(U32)
        topf = small[:, 2624:2656]
        best = small[:, 2656:2672]
        pos = small[:, 2672:2688].bitcast(U32)
        hilo = small[:, 2688:2720].bitcast(U32)
        hilof = small[:, 2720:2752]
        sel = small[:, 2752:2784]
        nbest = small[:, 2784:2786]
        esum = small[:, 2786:2788]
        rsum = small[:, 2788:2790]
        expv = small[:, 2790:2822].rearrange("p (a k) -> p a k", a=2)
        acol = small[:, 2822:2838].rearrange("p (a k) -> p a k", a=2)
        gcol = small[:, 2838:2854].rearrange("p (a k) -> p a k", a=2)
        wts = small[:, 2854:2870].rearrange("p (a k) -> p a k", a=2)
        idx = small[:, 2870:2902].bitcast(U32)

        def row(first, e):
            r = (first + e) % ROWS
            return ring[:, r * D:(r + 1) * D]

        u_ring = [row(UROW, e) for e in range(GROUP)]
        v_ring = [row(VROW, e) for e in range(GROUP)]

        def slot(b):
            return ring[:, SLOT[b] * KC * BLK:(SLOT[b] + 1) * KC * BLK]

        bank = [ctx.enter_context(nc.psum_tensor(f"bank{i}", [P, BLK], F32)) for i in range(8)]
        PIECE_BANKS = (0, 1)
        SCORE_BANKS = (2, 3)
        TURN_BANK, GATE_BANK, ATTN_BANK, COND_BANK = 4, 5, 6, 7
        UP_BANKS = ((0, 1, 4, 5), (4, 5, 2, 3))
        OUT_BANKS = ((2, 3), (4, 5))
        XT_BANKS, HT_BANKS = (2, 3, 4, 5), (6, 7)
        WT_BANKS = (2, 3, 4, 5, 6, 2)
        Q_BANK, QT_BANK = 0, 1
        ACC_BANKS = ((2, 3), (4, 5))

        x_in = sem("x_in")
        c_in = sem("c_in")
        bcond_in = [sem(f"bcond_in{i}") for i in range(2)]
        keys_in = sem("keys_in")
        spat_in = sem("spat_in")
        sgu_in = sem("sgu_in")
        brow_in = sem("brow_in")
        w_arrived = [sem(f"w_arrived{i}") for i in range(SLOTS)]
        ln1_in = sem("ln1_in")
        ln2_in = sem("ln2_in")
        wpq_in = [sem(f"wpq_in{i}") for i in range(2)]
        u_in = [sem(f"u_in{i}") for i in range(GROUP)]
        v_in = [sem(f"v_in{i}") for i in range(GROUP)]
        out_stored = sem("out_stored")

        consts = sem("consts")
        spat_masked = sem("spat_masked")
        dve_step = sem("dve_step")
        topk_step = sem("topk_step")
        silu_tanh = sem("silu_tanh")
        silu_done = sem("silu_done")
        var_ready = sem("var_ready")
        std_ready = sem("std_ready")
        xn_done = sem("xn_done")
        cacc_ready = sem("cacc_ready")
        cond_sum = sem("cond_sum")
        cond_saved = sem("cond_saved")
        xT_ready = sem("xT_ready")
        mod1_ready = sem("mod1_ready")
        wT_ready = sem("wT_ready")
        wT_saved = sem("wT_saved")
        hT_saved_act = sem("hT_saved_act")
        hT_saved_dve = sem("hT_saved_dve")
        h2T_ready = sem("h2T_ready")
        h2T_saved = sem("h2T_saved")
        piece_ready = sem("piece_ready")
        piece_saved = sem("piece_saved")
        gvar_ready = sem("gvar_ready")
        gstd_ready = sem("gstd_ready")
        vv_ready = sem("vv_ready")
        scores_ready = sem("scores_ready")
        max_ready = sem("max_ready")
        exp_done = sem("exp_done")
        probs_ready = sem("probs_ready")
        turned = sem("turned")
        turned_saved = sem("turned_saved")
        attn_ready = sem("attn_ready")
        attn_saved = sem("attn_saved")
        gate_ready = sem("gate_ready")
        gate_saved = sem("gate_saved")
        up_ready = sem("up_ready")
        merged = sem("merged")
        o_ready = sem("o_ready")
        h2_ready = sem("h2_ready")
        q_ready = sem("q_ready")
        q_saved = sem("q_saved")
        qT_ready = sem("qT_ready")
        qT_saved = sem("qT_saved")
        s_ready = sem("s_ready")
        s_saved = sem("s_saved")
        best_ready = sem("best_ready")
        idx_ready = sem("idx_ready")
        wexp_done = sem("wexp_done")
        rsum_ready = sem("rsum_ready")
        dots_done = sem("dots_done")
        gelu_done = sem("gelu_done")
        wts_ready = sem("wts_ready")
        diag_ready = sem("diag_ready")
        v_used = sem("v_used")
        out_ready = sem("out_ready")
        pool_turn = sem("pool_turn")
        dve_turn = sem("dve_turn")

        def hold(engine, turn, s, value):
            engine.wait_ge(s, value)
            engine.sem_inc(turn, 1)

        block = ctx.enter_context(nc.Block())

        @block.sync
        def _(sp):
            w_of = {
                "c": w_cond[0].rearrange("(p k) n -> p k n", k=KC),
                "in": w_in[0].rearrange("(k p) n -> p k n", p=P),
                "o": w_out[0].rearrange("(k p) n -> p k n", p=P),
            }
            up_of = {"ua": w_attn_up[0].rearrange("(k p) n -> p k n", p=P),
                     "ug": w_gmlp_up[0].rearrange("(k p) n -> p k n", p=P)}

            sp.dma_start(x_sb[:], x[0].rearrange("(t p) d -> p t d", p=P)).then_inc(x_in, 16)
            for n, b in enumerate(STREAM):
                kind, i = b
                if n >= SLOTS:
                    old, j = STREAM[n - SLOTS]
                    if old == "c":
                        sp.wait_ge(cacc_ready, j + 1)
                    elif old == "in":
                        sp.wait_ge(piece_ready, 2 * j + 2)
                    else:
                        sp.wait_ge(up_ready, KC)
                if kind in up_of:
                    sp.dma_start(slot(b).rearrange("p (k n) -> p k n", k=WC), up_of[kind]).then_inc(w_arrived[SLOT[b]], 16)
                else:
                    sp.dma_start(slot(b).rearrange("p (k n) -> p k n", k=KC),
                                 w_of[kind][:, :, i * BLK:(i + 1) * BLK]).then_inc(w_arrived[SLOT[b]], 16)
                if b == ("in", 0):
                    sp.dma_start(cond[:].rearrange("p a n -> p (a n)"),
                                 b_cond[0:1, 2 * D:6 * D].broadcast_to([P, 4 * D])).then_inc(bcond_in[1], 16)
                if b == ("c", 10):
                    for params, g, b_, landed in ((ln1, ln1_g, ln1_b, ln1_in), (ln2, ln2_g, ln2_b, ln2_in)):
                        sp.dma_start(params[:, LN_G, :], g[0:1, :].broadcast_to([P, D])).then_inc(landed, 16)
                        sp.dma_start(params[:, LN_B, :], b_[0:1, :].broadcast_to([P, D])).then_inc(landed, 16)
            wq_of = w_peer_q[0].rearrange("(k p) n -> p k n", p=P)
            for h in range(HEADS):
                if h == 0:
                    sp.wait_ge(attn_ready, HEADS)
                    sp.wait_ge(gate_ready, 2)
                if h == EARLY:
                    sp.wait_ge(merged, 4 * TILES)
                sp.dma_start(wpq[:, h * KC * 256:(h + 1) * KC * 256].rearrange("p (k n) -> p k n", k=KC),
                             wq_of[:, :, h * 256:(h + 1) * 256]).then_inc(wpq_in[int(h >= EARLY)], 16)
            for t in range(TILES):
                sp.wait_ge(out_ready, t + 1)
                sp.dma_start(out[0, t * P:(t + 1) * P, :], h_sb[:, t, :]).then_inc(out_stored, 16)
            sp.wait_ge(out_stored, 16 * TILES)

        @block.gpsimd
        def _(pool):
            nc.gpsimd.memset(ones[:], 1.0).then_inc(consts, 1)
            nc.gpsimd.memset(eps[:], EPS).then_inc(consts, 1)
            nc.gpsimd.memset(ident[:], 0.0).then_inc(consts, 1)
            nc.gpsimd.memset(zero_tile[:], 0.0).then_inc(consts, 1)
            nc.gpsimd.iota(iota_i[:, 0:P], pattern=[[1, P]], base=0, channel_multiplier=-1).then_inc(consts, 1)
            nc.gpsimd.iota(iota_i[:, P:3 * P], pattern=[[1, 2 * P]], base=-P, channel_multiplier=-1).then_inc(consts, 1)
            nc.gpsimd.iota(iota_i[:, 3 * P:3 * P + TOPK], pattern=[[1, TOPK]], base=0, channel_multiplier=0).then_inc(consts, 1)
            pool.wait_ge(consts, 7)
            nc.gpsimd.affine_select(out=ident[:], in_=ident[:], compare_op=ALU.not_equal, fill=1.0, base=0,
                                    pattern=[[-1, P]], channel_multiplier=1).then_inc(consts, 1)
            nc.gpsimd.tensor_copy(negdist, iota_i[:, 0:3 * P]).then_inc(consts, 1)
            nc.gpsimd.tensor_copy(iota16[:], iota_i[:, 3 * P:3 * P + TOPK]).then_inc(consts, 1)
            pool.wait_ge(consts, 10)
            nc.gpsimd.affine_select(out=negdist[:, 0:P], in_=negdist[:, 0:P], compare_op=ALU.is_ge, fill=FAR, base=0,
                                    pattern=[[-1, P]], channel_multiplier=1).then_inc(consts, 1)
            nc.gpsimd.affine_select(out=negdist[:, P:3 * P], in_=negdist[:, P:3 * P], compare_op=ALU.is_ge, fill=FAR,
                                    base=P, pattern=[[-1, 2 * P]], channel_multiplier=1).then_inc(consts, 1)
            pool.wait_ge(spat_in, 16)
            nc.gpsimd.affine_select(out=spat_nat, in_=spat_nat, compare_op=ALU.is_ge, fill=0.0, base=0,
                                    pattern=[[0, HEADS], [-1, P]], channel_multiplier=1).then_inc(spat_masked, 1)

            def gather_pair(i, a):
                p = 2 * i + a

                def gather(table, dst, e, k, landed):
                    nc.gpsimd.indirect_dma_start(
                        out=dst[e], out_offset=None, in_=table[0],
                        in_offset=bass.IndirectOffsetOnAxis(ap=idx[:, k:k + 1], axis=0)).then_inc(landed[e], 16)

                hold(pool, pool_turn, idx_ready, p + 1)
                for g in range(2):
                    n = 2 * p + g
                    first = a * TOPK + g * GROUP
                    hold(pool, pool_turn, dots_done, GROUP * n + GROUP)
                    for e in range(GROUP):
                        gather(peer_u, u_ring, e, first + e, u_in)
                    for e in range(GROUP):
                        if e % 2 == 0:
                            hold(pool, pool_turn, v_used, GROUP * n + e + 2)
                        gather(peer_v, v_ring, e, first + e, v_in)

            with pool.Fori(0, PAIRS // 2) as i:
                gather_pair(i, 0)
                gather_pair(i, 1)

        @block.scalar
        def _(act):
            act.dma_start(c_col[:, 0, :], c[0].rearrange("(p k) -> p k", k=KC)).then_inc(c_in, 16)
            act.dma_start(b1_row, b_cond[0:1, 0:2 * D]).then_inc(bcond_in[0], 16)
            act.wait_ge(c_in, 16)
            nc.scalar.activation(c_col[:, 1, :], c_col[:, 0, :], ACT.Tanh, scale=0.5).then_inc(silu_tanh, 1)

            def root(n):
                act.wait_ge(var_ready, n + 1)
                nc.scalar.activation(std[:, n, 0:1], moments[:, n, 1:2], ACT.Sqrt, bias=eps[:]).then_inc(std_ready, 1)

            act.wait_ge(consts, 2)
            root(0)
            root(1)

            act.wait_ge(mod1_ready, 2)
            act.dma_start(spat_nat, w_spatial[0].rearrange("g t s -> t g s")).then_inc(spat_in, 16)
            act.dma_start(brow, b_spatial[0:1].rearrange("a g t -> a (g t)")).then_inc(brow_in, 16)
            act.dma_start(keys_nat, peer_sub_keys[0].rearrange("h c n d -> n (h c) d")).then_inc(keys_in, 16)
            for i, v in enumerate((sgu_ln_g, sgu_ln_b)):
                act.dma_start(sgu_gb[:, i, :], v[0:1].rearrange("a g d -> a (g d)").broadcast_to([P, WIDTH])).then_inc(sgu_in, 16)

            def save_wT(n):
                act.wait_ge(wT_ready, n + 1)
                dst = spatT[:, 4 * n:4 * n + 4, :] if n < 2 else keysT[:, 4 * n - 8:4 * n - 4, :]
                nc.scalar.activation(dst.rearrange("p g t -> p (g t)"), bank[WT_BANKS[n]][:], ACT.Copy).then_inc(wT_saved, 1)

            act.wait_ge(xT_ready, 1)
            for r in (0, 2):
                for m in range(2):
                    k = 2 * r + m
                    nc.scalar.activation(hT[:, k, :], bank[XT_BANKS[r]][:, m * SEQ:(m + 1) * SEQ], ACT.Identity,
                                         scale=mod1[:, 1, k:k + 1], bias=mod1[:, 0, k:k + 1]).then_inc(hT_saved_act, 1)

            def save_h2T(t):
                act.wait_ge(h2T_ready, t + 1)
                for r in range(2):
                    nc.scalar.activation(hT[:, 4 * r:4 * r + 4, t * P:(t + 1) * P],
                                         bank[HT_BANKS[r]][:].rearrange("p (k n) -> p k n", n=P), ACT.Copy).then_inc(h2T_saved, 1)

            def piece(n):
                b, half = n // 2, n % 2
                act.wait_ge(piece_ready, n + 1)
                src = bank[PIECE_BANKS[n % 2]][:]
                two = slice(2 * half, 2 * half + 2)
                if b == IN_Q:
                    ins = nc.scalar.activation(qT[:, two, :].rearrange("p c t -> p (c t)"), src, ACT.Copy, scale=HD ** -0.5)
                elif b == IN_K:
                    ins = nc.scalar.activation(kT[:, two, :].rearrange("p c t -> p (c t)"), src, ACT.Copy)
                elif b == IN_V:
                    ins = nc.scalar.activation(v_sb[:, half, :], src, ACT.Copy)
                elif b == IN_GU:
                    ins = nc.scalar.activation(uT[:, two, :].rearrange("p c t -> p (c t)"), src, ACT.Gelu)
                elif b == IN_GV:
                    ins = nc.scalar.activation(gv[:, half, :], src, ACT.Gelu)
                else:
                    which = int(b >= IN_GG)
                    first = 4 * (b - (IN_GG if which else IN_GA)) + 2 * half
                    ins = nc.scalar.activation(gates_v[:, :, first:first + 2, which, :],
                                               src.rearrange("p (c t n) -> p t c n", c=2, t=TILES), ACT.Tanh, scale=0.5)
                ins.then_inc(piece_saved, 1)

            for n in range(2 * IN_GA):
                piece(n)
                if n == 1:
                    save_wT(0)
                    save_wT(1)
                if n == 3:
                    for m in range(2, 6):
                        save_wT(m)
            act.wait_ge(gvar_ready, 1)
            nc.scalar.activation(gst[:, 2, :], gst[:, 1, :], ACT.Sqrt, bias=eps[:], scale=1.0 / HD).then_inc(gstd_ready, 1)

            for j in range(HEADS + 2):
                if j < HEADS:
                    for t in range(TILES):
                        act.wait_ge(max_ready, 2 * j + t + 1)
                        cols = slice(0, P) if t == 0 else slice(P, 3 * P)
                        nc.scalar.activation(probs[:, j % 2, cols], probs[:, j % 2, cols], ACT.Exp, bias=amax[:, j, t:t + 1],
                                             accum_out=asum[:, 0, j, t:t + 1]).then_inc(exp_done, 1)
                    piece(2 * IN_GA + j)
                if 1 <= j <= HEADS:
                    act.wait_ge(turned, j)
                    if j >= 3:
                        act.wait_ge(attn_ready, j - 2)
                    nc.scalar.activation(probsT[:, (j - 1) % 2, :], bank[TURN_BANK][:, 0:3 * P], ACT.Copy).then_inc(turned_saved, 1)
                if j >= 3 and j % 2 == 1:
                    m = (j - 3) // 2
                    act.wait_ge(attn_ready, 2 * m + 2)
                    nc.scalar.activation(attnT[:, m, :], bank[ATTN_BANK][:, (m % 2) * SEQ:(m % 2 + 1) * SEQ],
                                         ACT.Copy).then_inc(attn_saved, 1)

            def save_scores(p):
                act.wait_ge(q_ready, p + 1)
                nc.scalar.activation(q_tok, bank[Q_BANK][:, 0:256], ACT.Copy).then_inc(q_saved, 1)
                act.wait_ge(qT_ready, p + 1)
                nc.scalar.activation(qTs.rearrange("p c t -> p (c t)"), bank[QT_BANK][:, 0:256], ACT.Copy).then_inc(qT_saved, 1)
                act.wait_ge(s_ready, p + 1)
                nc.scalar.activation(sc, bank[QT_BANK][:, 256:512], ACT.Copy).then_inc(s_saved, 1)

            def softmax_exp(p, a):
                act.wait_ge(best_ready, p + 1)
                nc.scalar.activation(expv[:, a, :], best, ACT.Exp, bias=nbest[:, a:a + 1],
                                     accum_out=esum[:, a:a + 1]).then_inc(wexp_done, 1)

            def weigh(i, a, following=True):
                p = 2 * i + a
                if following:
                    save_scores(p + 1)
                for g in range(2):
                    n = 2 * p + g
                    act.wait_ge(dots_done, GROUP * n + 2 * GROUP)
                    nc.scalar.activation(gcol[:, g, :], acol[:, g, :], ACT.Gelu).then_inc(gelu_done, 1)
                    act.wait_ge(wts_ready, n + 1)
                    for e in range(GROUP):
                        if e % 2 == 0:
                            act.wait_ge(v_used, GROUP * n + e + 2)
                        nc.scalar.activation(diag[:, e, :], ident[:], ACT.Copy, scale=wts[:, g, e:e + 1]).then_inc(diag_ready, 1)
                    if g == 0 and following:
                        softmax_exp(p + 1, 1 - a)

            root(2)
            root(3)
            save_h2T(0)
            save_scores(0)
            softmax_exp(0, 0)
            weigh(0, 0)
            root(4)
            root(5)
            weigh(0, 1)
            save_h2T(1)
            with act.Fori(1, PAIRS // 2 - 1) as i:
                weigh(i, 0)
                weigh(i, 1)
            root(6)
            weigh(PAIRS // 2 - 1, 0)
            weigh(PAIRS // 2 - 1, 1, following=False)
            root(7)

        @block.vector
        def _(dve):
            steps = [0]

            def link(ins):
                steps[0] += 1
                ins.then_inc(dve_step, 1)
                dve.wait_ge(dve_step, steps[0])

            V = nc.vector

            def variance(n, src):
                for i in range(2):
                    last = V.bn_stats(stats[:, n, i, :], src[:, i * BLK:(i + 1) * BLK])
                    if i == 0:
                        last.then_inc(dve_step, 1)
                        steps[0] += 1
                link(last)
                V.bn_aggr(moments[:, n, :], stats[:, n, :, :].rearrange("p a b -> p (a b)")).then_inc(var_ready, 1)

            def normalise(n, dst, src):
                dve.wait_ge(std_ready, n + 1)
                link(V.reciprocal(std[:, n, 1:2], std[:, n, 0:1]))
                return V.tensor_scalar(dst, src, moments[:, n, 0:1], std[:, n, 1:2], ALU.subtract, ALU.mult)

            dve.wait_ge(x_in, 16)
            for t in range(TILES):
                variance(t, x_sb[:, t, :])
            dve.wait_ge(silu_tanh, 1)
            link(V.scalar_tensor_tensor(out=c_col[:, 2, :], in0=c_col[:, 1, :], scalar=1.0, in1=c_col[:, 0, :],
                                        op0=ALU.add, op1=ALU.mult))
            link(V.tensor_scalar(c_col[:, 2, :], c_col[:, 2, :], 0.5, None, ALU.mult))
            for t in range(TILES):
                normalise(t, h_sb[:, t, :], x_sb[:, t, :]).then_inc(xn_done, 1)

            def cond_block(n):
                b = ("c", n)
                dve.wait_ge(w_arrived[SLOT[b]], 16 * (TURN[b] + 1))
                if n >= 2:
                    dve.wait_ge(cond_sum, n - 1)
                w = slot(b).rearrange("p (k n) -> p k n", k=KC)
                acc = cacc[:, n % 2, :]
                link(V.tensor_scalar(acc, w[:, 0, :], c_col[:, 2, 0:1], None, ALU.mult))
                for k in range(1, KC):
                    ins = V.scalar_tensor_tensor(out=acc, in0=w[:, k, :], scalar=c_col[:, 2, k:k + 1], in1=acc,
                                                 op0=ALU.mult, op1=ALU.add)
                    if k < KC - 1:
                        link(ins)
                ins.then_inc(cacc_ready, 1)

            def cond_save(n):
                dve.wait_ge(cond_sum, n + 1)
                row = n // 2 - 2
                part = cond[:, row, (n % 2) * BLK:(n % 2 + 1) * BLK]
                one = 0.0 if row == SH2 else 1.0
                V.scalar_tensor_tensor(out=part, in0=bank[COND_BANK][:], scalar=one, in1=part,
                                       op0=ALU.add, op1=ALU.add).then_inc(cond_saved, 1)

            for n in range(4):
                cond_block(n)
            dve.wait_ge(cond_sum, 4)
            V.tensor_copy(mod1[:, 0, :], bank[COND_BANK][:, 0:KC]).then_inc(mod1_ready, 1)
            V.tensor_scalar(mod1[:, 1, :], bank[COND_BANK][:, KC:2 * KC], 1.0, None, ALU.add).then_inc(mod1_ready, 1)
            dve.wait_ge(mod1_ready, 2)
            dve.wait_ge(xT_ready, 1)
            for r in (1, 3):
                for m in range(2):
                    k = 2 * r + m
                    V.tensor_scalar(hT[:, k, :], bank[XT_BANKS[r]][:, m * SEQ:(m + 1) * SEQ], mod1[:, 1, k:k + 1],
                                    mod1[:, 0, k:k + 1], ALU.mult, ALU.add).then_inc(hT_saved_dve, 1)

            dve.wait_ge(bcond_in[1], 16)
            for n in range(4, 9):
                cond_block(n)
                if n > 4:
                    cond_save(n - 1)
            cond_save(8)

            def wide(v):
                return v.unsqueeze(2).broadcast_to([P, 2 * HEADS, HD])

            sq = scratch.rearrange("p (g n) -> p g n", n=HD)
            dve.wait_ge(piece_saved, 2 * IN_GV + 2)
            link(V.tensor_reduce(gst[:, 0, :], gv_g, AX_X, ALU.add))
            link(V.tensor_scalar(gst[:, 0, :], gst[:, 0, :], 1.0 / HD, None, ALU.mult))
            link(V.tensor_tensor(gv_g, gv_g, wide(gst[:, 0, :]), ALU.subtract))
            link(V.tensor_tensor(sq, gv_g, gv_g, ALU.mult))
            V.tensor_reduce(gst[:, 1, :], sq, AX_X, ALU.add).then_inc(gvar_ready, 1)
            dve.wait_ge(gstd_ready, 1)
            link(V.reciprocal(gst[:, 3, :], gst[:, 2, :]))
            link(V.tensor_tensor(gv_g, gv_g, wide(gst[:, 3, :]), ALU.mult))
            dve.wait_ge(sgu_in, 32)
            for i, op in ((0, ALU.mult), (1, ALU.add)):
                ins = V.tensor_tensor(gv, gv, sgu_gb[:, i, :].unsqueeze(1).broadcast_to([P, TILES, WIDTH]), op)
                if i == 0:
                    link(ins)
            ins.then_inc(vv_ready, 1)

            def save_gate(r):
                dve.wait_ge(gate_ready, r + 1)
                part = uT[:, 2 * r:2 * r + 2, :].rearrange("p c t -> p (c t)")
                V.tensor_tensor(part, part, bank[GATE_BANK][:], ALU.mult).then_inc(gate_saved, 1)

            dve.wait_ge(consts, 12)
            for j in range(HEADS):
                pj = probs[:, j % 2, :]
                if j >= 2:
                    dve.wait_ge(turned, j - 1)
                dve.wait_ge(scores_ready, j + 1)
                link(V.scalar_tensor_tensor(out=pj, in0=negdist, scalar=2.0 ** -(j + 1), in1=bank[SCORE_BANKS[j % 2]][:, 0:3 * P],
                                            op0=ALU.mult, op1=ALU.add))
                for t in range(TILES):
                    cols = slice(0, P) if t == 0 else slice(P, 3 * P)
                    V.tensor_reduce(amax[:, j, t:t + 1], pj[:, cols], AX_X, ALU.max, negate=True).then_inc(max_ready, 1)
                dve.wait_ge(exp_done, 2 * j + 2)
                link(V.reciprocal(asum[:, 1, j, :], asum[:, 0, j, :]))
                for t in range(TILES):
                    cols = slice(0, P) if t == 0 else slice(P, 3 * P)
                    V.tensor_scalar(pj[:, cols], pj[:, cols], asum[:, 1, j, t:t + 1], None, ALU.mult).then_inc(probs_ready, 1)
                if j in (0, 2, 4):
                    cond_block(9 + j // 2)
                if j in (3, 5, 7):
                    cond_save(8 + j // 2)
                if j == 5:
                    save_gate(0)
            save_gate(1)

            def merge(t):
                tmp = scratch[:, 0:BLK]
                for r in range(KC // 2):
                    n = (KC // 2) * t + r
                    dve.wait_ge(up_ready, n + 1)
                    if n:
                        dve.wait_ge(merged, n)
                    g0 = (t * KC + 2 * r) * 2 * P
                    link(V.scalar_tensor_tensor(out=tmp, in0=gates[:, g0:g0 + BLK], scalar=1.0, in1=bank[UP_BANKS[t][r]][:],
                                                op0=ALU.add, op1=ALU.mult))
                    halves = tmp.rearrange("p (k a n) -> p k a n", k=2, a=2)
                    V.tensor_tensor(hT[:, 2 * r:2 * r + 2, t * P:(t + 1) * P], halves[:, :, 0, :], halves[:, :, 1, :],
                                    ALU.add).then_inc(merged, 1)

            dve.wait_ge(piece_saved, PIECES)
            merge(0)

            def residual(t, banks, gate, halve, dst):
                for i in range(2):
                    cols = slice(i * BLK, (i + 1) * BLK)
                    ins = V.scalar_tensor_tensor(out=dst[:, cols], in0=bank[banks[i]][:], scalar=halve,
                                                 in1=cond[:, gate, cols], op0=ALU.mult, op1=ALU.mult)
                    ins.then_inc(dve_step, 1)
                    steps[0] += 1
                dve.wait_ge(dve_step, steps[0])
                link(V.scalar_tensor_tensor(out=dst, in0=x_sb[:, t, :], scalar=ALPHA, in1=dst, op0=ALU.mult, op1=ALU.add))

            TOPK_STEPS = 23

            class Steps:

                def __init__(self, p, n):
                    self.p, self.n = p, n

                def __call__(self, *many):
                    for ins in many:
                        self.n += 1
                        ins.then_inc(topk_step, 1)
                    hold(dve, dve_turn, topk_step, self.p * TOPK_STEPS + self.n)

            HALF_STEPS = 11

            def topk_halves(p):
                step = Steps(p, 0)
                hold(dve, dve_turn, s_saved, p + 1)
                half = [slice(0, NKEYS), slice(NKEYS, 2 * NKEYS)]
                hi8 = [slice(0, 8), slice(TOPK, TOPK + 8)]
                lo8 = [slice(8, TOPK), slice(TOPK + 8, 2 * TOPK)]
                step(*[V.max(top[:, hi8[c]], sc[:, half[c]]) for c in range(2)])
                step(*[V.match_replace(sr[:, half[c]], top[:, hi8[c]], sc[:, half[c]], LOWEST) for c in range(2)],
                     *[V.max_index(topi[:, hi8[c]], top[:, hi8[c]], sc[:, half[c]]) for c in range(2)])
                step(*[V.max(top[:, lo8[c]], sr[:, half[c]]) for c in range(2)])
                step(*[V.max_index(topi[:, lo8[c]], top[:, lo8[c]], sr[:, half[c]]) for c in range(2)],
                     V.tensor_tensor(cand.rearrange("p (i j) -> p i j", i=TOPK),
                                     top[:, 0:TOPK].unsqueeze(2).broadcast_to([P, TOPK, TOPK]),
                                     top[:, TOPK:2 * TOPK].unsqueeze(1).broadcast_to([P, TOPK, TOPK]), ALU.add))
                assert step.n == HALF_STEPS, step.n

            def topk_sums(p, a):
                step = Steps(p, HALF_STEPS)
                step(V.max(best[:, 0:8], cand))
                step(V.match_replace(candr, best[:, 0:8], cand, LOWEST),
                     V.max_index(pos[:, 0:8], best[:, 0:8], cand),
                     V.tensor_scalar(nbest[:, a:a + 1], best[:, 0:1], -1.0, None, ALU.mult))
                V.max(best[:, 8:TOPK], candr).then_inc(best_ready, 1)
                hold(dve, dve_turn, best_ready, p + 1)
                step(V.max_index(pos[:, 8:TOPK], best[:, 8:TOPK], candr),
                     V.tensor_copy(topf, topi))
                step(V.tensor_scalar(hilo[:, 0:TOPK], pos, SHIFT, None, ALU.logical_shift_right),
                     V.tensor_scalar(hilo[:, TOPK:2 * TOPK], pos, MASK, None, ALU.bitwise_and))
                step(V.tensor_copy(hilof, hilo))
                oh = onehot.rearrange("p (m i) -> p m i", i=TOPK)
                oh4 = onehot.rearrange("p (c k i) -> p c k i", c=2, k=TOPK)
                step(V.tensor_tensor(oh, hilof.unsqueeze(2).broadcast_to([P, 2 * TOPK, TOPK]),
                                     iota16[:].unsqueeze(1).broadcast_to([P, 2 * TOPK, TOPK]), ALU.is_equal))
                step(V.tensor_tensor(oh4, oh4, topf.rearrange("p (c i) -> p c i", c=2).unsqueeze(2)
                                     .broadcast_to([P, 2, TOPK, TOPK]), ALU.mult))
                step(V.tensor_reduce(sel, oh, AX_X, ALU.add))
                assert step.n == TOPK_STEPS, step.n
                if not (isinstance(p, int) and p == 0):
                    hold(dve, dve_turn, v_used, p * TOPK - TOPK + GROUP)
                V.scalar_tensor_tensor(out=idx[:, a * TOPK:(a + 1) * TOPK], in0=sel[:, 0:TOPK], scalar=float(NKEYS),
                                       in1=sel[:, TOPK:2 * TOPK], op0=ALU.mult, op1=ALU.add).then_inc(idx_ready, 1)

            def weights(p, a, g):
                if g == 0:
                    dve.wait_ge(wexp_done, p + 1)
                    V.reciprocal(rsum[:, a:a + 1], esum[:, a:a + 1]).then_inc(rsum_ready, 1)
                dve.wait_ge(rsum_ready, p + 1)
                dve.wait_ge(gelu_done, 2 * p + g + 1)
                V.scalar_tensor_tensor(out=wts[:, g, :], in0=gcol[:, g, :], scalar=rsum[:, a:a + 1],
                                       in1=expv[:, a, g * GROUP:(g + 1) * GROUP], op0=ALU.mult, op1=ALU.mult).then_inc(wts_ready, 1)

            def dots(i, a, t, following=True):
                p = 2 * i + a
                for g in range(2):
                    for e in range(GROUP):
                        dve.wait_ge(u_in[e], 16 * (2 * p + g + 1))
                        V.tensor_tensor_reduce(u_ring[e], u_ring[e], h_sb[:, t, :], 1.0, 0.0, ALU.mult, ALU.add,
                                               acol[:, g, e:e + 1]).then_inc(dots_done, 1)
                    if g == 0 and following:
                        topk_halves(p + 1)
                    weights(p, a, g)
                    if g == 0 and following:
                        topk_sums(p + 1, 1 - a)

            def norm_and_modulate(t):
                ht, xt = h_sb[:, t, :], x_sb[:, t, :]
                dve.wait_ge(o_ready, t + 1)
                residual(t, OUT_BANKS[t], GT1, 0.5, ht)
                variance(2 + 2 * t, ht)
                link(normalise(2 + 2 * t, xt, ht))
                link(V.tensor_tensor(xt, xt, ln1[:, LN_G, :], ALU.mult))
                link(V.tensor_tensor(xt, xt, ln1[:, LN_B, :], ALU.add))
                variance(3 + 2 * t, xt)
                link(normalise(3 + 2 * t, ht, xt))
                link(V.tensor_tensor(ht, ht, cond[:, SC2, :], ALU.mult))
                V.tensor_tensor(ht, ht, cond[:, SH2, :], ALU.add).then_inc(h2_ready, 1)

            def finish(t):
                ht = h_sb[:, t, :]
                dve.wait_ge(v_used, GROUP + HEADS * TOPK * (t + 1))
                residual(t, ACC_BANKS[t], GT2, 1.0, ht)
                variance(6 + t, ht)
                link(normalise(6 + t, ht, ht))
                link(V.tensor_tensor(ht, ht, ln2[:, LN_G, :], ALU.mult))
                V.tensor_tensor(ht, ht, ln2[:, LN_B, :], ALU.add).then_inc(out_ready, 1)

            dve.wait_ge(ln1_in, 32)
            dve.wait_ge(cond_saved, 8)
            norm_and_modulate(0)
            merge(1)
            dve.sem_inc(dots_done, GROUP)
            topk_halves(0)
            topk_sums(0, 0)
            dots(0, 0, 0)
            norm_and_modulate(1)
            dots(0, 1, 0)
            with dve.Fori(1, HEADS // 2) as i:
                dots(i, 0, 0)
                dots(i, 1, 0)
            dve.wait_ge(h2_ready, TILES)
            with dve.Fori(HEADS // 2, PAIRS // 2 - 1) as i:
                dots(i, 0, 1)
                dots(i, 1, 1)
            dve.wait_ge(ln2_in, 32)
            finish(0)
            dots(PAIRS // 2 - 1, 0, 1)
            dots(PAIRS // 2 - 1, 1, 1, following=False)
            finish(1)

        @block.tensor
        def _(pe):
            T = nc.tensor
            pe.wait_ge(consts, 8)

            for t in range(TILES):
                pe.wait_ge(xn_done, t + 1)
                for k in range(KC):
                    last = T.transpose(bank[XT_BANKS[k // 2]][:, k % 2 * SEQ + t * P:k % 2 * SEQ + (t + 1) * P],
                                       h_sb[:, t, k * P:(k + 1) * P], ident[:])
            last.then_inc(xT_ready, 1)

            def cond_columns(n):
                pe.wait_ge(cacc_ready, n + 1)
                for m in range(BLK // P):
                    k = n * (BLK // P) + m
                    T.matmul(bank[COND_BANK][:, k:k + 1], cacc[:, n % 2, m * P:(m + 1) * P], ones[:, 0:1], start=True, stop=False)
                    last = T.matmul(bank[COND_BANK][:, k:k + 1], b1_row[:, k * P:(k + 1) * P], ones[0:1, 0:1], start=False, stop=True)
                last.then_inc(cond_sum, 1)

            pe.wait_ge(bcond_in[0], 16)
            for n in range(4):
                cond_columns(n)

            def cond_total(n):
                pe.wait_ge(cacc_ready, n + 1)
                if n > 4:
                    pe.wait_ge(cond_saved, n - 4)
                T.matmul(bank[COND_BANK][:], ones[:], cacc[:, n % 2, :], start=True, stop=True).then_inc(cond_sum, 1)

            def turn_weights(n):
                if n == 5:
                    pe.wait_ge(wT_saved, 1)
                for g in range(4):
                    src = spat_nat[:, 4 * n + g, :] if n < 2 else keys_nat[:, 4 * n - 8 + g, :]
                    last = T.transpose(bank[WT_BANKS[n]][:, g * P:(g + 1) * P], src, ident[:])
                last.then_inc(wT_ready, 1)

            def arrived(b):
                pe.wait_ge(w_arrived[SLOT[b]], 16 * (TURN[b] + 1))

            def piece(n):
                b, half = n // 2, n % 2
                w = slot(("in", b)).rearrange("p (k n) -> p k n", k=KC)
                if half == 0:
                    arrived(("in", b))
                if n >= 2:
                    pe.wait_ge(piece_saved, n - 1)
                dst = bank[PIECE_BANKS[n % 2]]
                if b in (IN_V, IN_GV):
                    for k in range(KC):
                        last = T.matmul(dst[:], hT[:, k, half * P:(half + 1) * P], w[:, k, :], start=(k == 0), stop=(k == KC - 1))
                else:
                    for m in range(2):
                        col = (2 * half + m) * P
                        for k in range(KC):
                            last = T.matmul(dst[:, m * SEQ:(m + 1) * SEQ], w[:, k, col:col + P], hT[:, k, :],
                                            start=(k == 0), stop=(k == KC - 1))
                last.then_inc(piece_ready, 1)

            pe.wait_ge(hT_saved_act, 4)
            pe.wait_ge(hT_saved_dve, 4)
            for b in range(IN_GA):
                piece(2 * b)
                piece(2 * b + 1)
                if b == 0:
                    pe.wait_ge(spat_masked, 1)
                    turn_weights(0)
                    turn_weights(1)
                if b == 1:
                    pe.wait_ge(keys_in, 16)
                    for n in range(2, 6):
                        turn_weights(n)
                cond_total(4 + b)

            def scores(j):
                rows = slice(HD * (j % 2), HD * (j % 2) + HD)
                if j == 0:
                    pe.wait_ge(wT_saved, 6)
                if j >= 2:
                    pe.wait_ge(max_ready, 2 * j - 2)
                dst = bank[SCORE_BANKS[j % 2]]
                T.matmul(dst[:, 0:P], qT[rows, j // 2, 0:P], kT[rows, j // 2, 0:P], start=True, stop=True)
                T.matmul(dst[:, P:3 * P], qT[rows, j // 2, P:SEQ], kT[rows, j // 2, :], start=True, stop=True).then_inc(scores_ready, 1)

            def turn(j):
                pe.wait_ge(probs_ready, 2 * j + 2)
                if j:
                    pe.wait_ge(turned_saved, j)
                for m in range(3):
                    last = T.transpose(bank[TURN_BANK][:, m * P:(m + 1) * P], probs[:, j % 2, m * P:(m + 1) * P], ident[:])
                last.then_inc(turned, 1)

            def attend(j):
                pe.wait_ge(turned_saved, j + 1)
                if j % 2 == 0 and j >= 2:
                    pe.wait_ge(attn_saved, j // 2)
                rows = slice(HD * (j % 2), HD * (j % 2) + HD)
                col = (j // 2 % 2) * SEQ
                dst = bank[ATTN_BANK]
                vh = [v_sb[:, t, j * HD:(j + 1) * HD] for t in range(TILES)]
                pt = probsT[:, j % 2, :]
                T.matmul(dst[rows, col:col + P], vh[0], pt[:, 0:P], start=True, stop=True)
                T.matmul(dst[rows, col + P:col + SEQ], vh[0], pt[:, P:2 * P], start=True, stop=False)
                T.matmul(dst[rows, col + P:col + SEQ], vh[1], pt[:, 2 * P:3 * P], start=False, stop=True).then_inc(attn_ready, 1)

            def spatial(r):
                if r == 0:
                    pe.wait_ge(vv_ready, 1)
                    pe.wait_ge(brow_in, 16)
                else:
                    pe.wait_ge(gate_saved, r)
                for g in range(4 * r, 4 * r + 4):
                    rows = slice(HD * (g % 2), HD * (g % 2) + HD)
                    for t in range(TILES):
                        col = (g // 2 % 2) * SEQ + t * P
                        dst = bank[GATE_BANK][rows, col:col + P]
                        T.matmul(dst, gv[:, t, g * HD:(g + 1) * HD], spatT[:, g, :], start=True, stop=False)
                        last = T.matmul(dst, ones[0:1, 0:HD], brow[:, g * P:(g + 1) * P], start=False, stop=True)
                last.then_inc(gate_ready, 1)

            for j in range(HEADS + 2):
                if j < HEADS:
                    scores(j)
                    piece(2 * IN_GA + j)
                if 1 <= j <= HEADS:
                    turn(j - 1)
                if j >= 2:
                    attend(j - 2)
                if j in (2, 4, 6):
                    cond_total(8 + j // 2)
                if j in (4, 6):
                    spatial(j // 2 - 2)

            ups = [(slot((kind, 0)).rearrange("p (k n) -> p k n", k=WC), src) for kind, src in (("ua", attnT), ("ug", uT))]

            def up(t):
                for r in range(KC // 2):
                    if t == 1 and r == 2:
                        pe.wait_ge(var_ready, 3)
                    for k2 in range(2):
                        n = 2 * r + k2
                        for m, (w, src) in enumerate(ups):
                            for k in range(WC):
                                last = T.matmul(bank[UP_BANKS[t][r]][:, (2 * k2 + m) * P:(2 * k2 + m + 1) * P],
                                                w[:, k, n * P:(n + 1) * P], src[:, k, t * P:(t + 1) * P],
                                                start=(k == 0), stop=(k == WC - 1))
                    last.then_inc(up_ready, 1)

            def project(t):
                pe.wait_ge(merged, KC // 2 * (t + 1))
                for m in range(2):
                    arrived(("o", m))
                    w = slot(("o", m)).rearrange("p (k n) -> p k n", k=KC)
                    for k in range(KC):
                        last = T.matmul(bank[OUT_BANKS[t][m]][:], hT[:, k, t * P:(t + 1) * P], w[:, k, :],
                                        start=(k == 0), stop=(k == KC - 1))
                last.then_inc(o_ready, 1)

            def transpose_h(t):
                pe.wait_ge(h2_ready, t + 1)
                for k in range(KC):
                    last = T.transpose(bank[HT_BANKS[k // 4]][:, k % 4 * P:(k % 4 + 1) * P], h_sb[:, t, k * P:(k + 1) * P], ident[:])
                last.then_inc(h2T_ready, 1)

            def retrieve(p, t):
                h = p - HEADS * t
                for k in range(KC):
                    last = T.matmul(bank[Q_BANK][:, 0:256], hT[:, k, t * P:(t + 1) * P],
                                    wpq[:, bass.ds((h * KC + k) * 256, 256)], start=(k == 0), stop=(k == KC - 1))
                last.then_inc(q_ready, 1)
                pe.wait_ge(q_saved, p + 1)
                for m in range(2):
                    last = T.transpose(bank[QT_BANK][:, m * P:(m + 1) * P], q_tok[:, m * P:(m + 1) * P], ident[:])
                last.then_inc(qT_ready, 1)
                pe.wait_ge(qT_saved, p + 1)
                for m in range(2):
                    last = T.matmul(bank[QT_BANK][:, (2 + m) * P:(3 + m) * P], qTs[:, m, :],
                                    keysT[:].rearrange("p m n -> p (m n)")[:, bass.ds((2 * h + m) * NKEYS, NKEYS)],
                                    start=True, stop=True)
                last.then_inc(s_ready, 1)

            def clear(t):
                for m in range(2):
                    last = T.matmul(bank[ACC_BANKS[t][m]][:, 0:BLK], zeros, h_sb[:, t, m * BLK:(m + 1) * BLK], start=True,
                                    stop=False, skip_group_check=True)
                return last

            def add_rows(i, a, t, following=None):
                p = 2 * i + a
                if following is not None:
                    pe.wait_ge(s_saved, p + 1)
                    retrieve(p + 1, following)
                for g in range(2):
                    n = 2 * p + g
                    for e in range(GROUP):
                        pe.wait_ge(v_in[e], 16 * (n + 1))
                        pe.wait_ge(diag_ready, GROUP * n + e + 1)
                        end = isinstance(p, int) and p % HEADS == HEADS - 1 and (g, e) == (1, GROUP - 1)
                        for m in range(2):
                            last = T.matmul(bank[ACC_BANKS[t][m]][:], diag[:, e, :], v_ring[e][:, m * BLK:(m + 1) * BLK],
                                            start=False, stop=end, skip_group_check=True)
                        last.then_inc(v_used, 1)

            zeros = zero_tile[:]
            arrived(("ua", 0))
            arrived(("ug", 0))
            pe.wait_ge(gate_saved, 2)
            pe.wait_ge(attn_saved, WC)
            pe.wait_ge(piece_saved, PIECES)
            up(0)
            project(0)
            up(1)
            transpose_h(0)
            pe.wait_ge(h2T_saved, 2)
            pe.wait_ge(wpq_in[0], 16 * EARLY)
            retrieve(0, 0)
            project(1)
            clear(0).then_inc(v_used, GROUP)
            add_rows(0, 0, 0, following=0)
            add_rows(0, 1, 0, following=0)
            transpose_h(1)
            clear(1)
            pe.wait_ge(wpq_in[1], 16 * (HEADS - EARLY))
            with pe.Fori(1, HEADS // 2 - 1) as i:
                add_rows(i, 0, 0, following=0)
                add_rows(i, 1, 0, following=0)
            pe.wait_ge(h2T_saved, 4)
            add_rows(HEADS // 2 - 1, 0, 0, following=0)
            add_rows(HEADS // 2 - 1, 1, 0, following=1)
            with pe.Fori(HEADS // 2, PAIRS // 2 - 1) as i:
                add_rows(i, 0, 1, following=1)
                add_rows(i, 1, 1, following=1)
            add_rows(PAIRS // 2 - 1, 0, 1, following=1)
            add_rows(PAIRS // 2 - 1, 1, 1)


_INS = ['x', 'c', 'w_cond', 'b_cond', 'w_in', 'w_attn_up', 'w_gmlp_up', 'w_out', 'sgu_ln_g', 'sgu_ln_b',
        'w_spatial', 'b_spatial', 'ln1_g', 'ln1_b', 'w_peer_q', 'peer_sub_keys', 'peer_u', 'peer_v', 'ln2_g', 'ln2_b']


def kernel(**inputs):
    import numpy as _np
    import concourse.bacc as _bacc
    from concourse import mybir as _mybir
    from concourse.bass_utils import run_bass_kernel_spmd as _run

    nc = _bacc.Bacc("TRN2", target_bir_lowering=False, num_devices=1)
    arrays, args = {}, []
    for name in _INS:
        a = _np.ascontiguousarray(inputs[name])
        arrays[f"in_{name}_dram"] = a
        args.append(nc.dram_tensor(f"in_{name}_dram", a.shape, _mybir.dt.from_np(a.dtype), kind="ExternalInput").ap())
    out = nc.dram_tensor("out_0_dram", (1, SEQ, D), F32, kind="ExternalOutput").ap()
    build(nc, *args, out)
    r = _run(nc, [arrays], core_ids=[0])
    return r.results[0]["out_0_dram"]
```

```python
from contextlib import ExitStack

import concourse.bass as bass
from concourse import mybir

F32 = mybir.dt.float32
I32 = mybir.dt.int32
U32 = mybir.dt.uint32
ALU = mybir.AluOpType
ACT = mybir.ActivationFunctionType
AX_X = mybir.AxisListType.X

P = 128
SEQ = 256
D = 1024
TILES = SEQ // P
KC = D // P
HEADS = 8
HD = 64
WIDTH = HEADS * HD
WC = WIDTH // P
BLK = 512
SLOTS = 4
PAIRS = TILES * HEADS
NKEYS = 128
TOPK = 16
GROUP = 8
SHIFT, MASK = 4, TOPK - 1
ALPHA = 2.0 ** 0.25
EPS = 1e-5
LOWEST = -3.0e38
FAR = -1.0e30

STREAM = [("c", 0), ("c", 1), ("c", 2), ("c", 3), ("in", 0), ("in", 1), ("c", 4), ("in", 2), ("c", 5), ("c", 6),
          ("in", 3), ("c", 7), ("in", 4), ("c", 8), ("in", 5), ("c", 9), ("in", 6), ("c", 10), ("in", 7), ("c", 11),
          ("in", 8), ("ua", 0), ("ug", 0), ("o", 0), ("o", 1)]
SLOT = {b: n % SLOTS for n, b in enumerate(STREAM)}
TURN = {b: n // SLOTS for n, b in enumerate(STREAM)}
IN_Q, IN_K, IN_V, IN_GU, IN_GV, IN_GA, IN_GG = 0, 1, 2, 3, 4, 5, 7
PIECES = 18
TE_ROWS = {0: 2, 1: 2, 2: 2, 3: 1}
DVE_ROWS = (1, 3, 5)
PE_ROWS = tuple(e for e in range(GROUP) if e not in DVE_ROWS)
GT1, SH2, SC2, GT2 = range(4)
LN_G, LN_B = 0, 1
UROW, VROW, ROWS = 4, 12, 16


def build(nc, x, c, w_cond, b_cond, w_in, w_attn_up, w_gmlp_up, w_out, sgu_ln_g, sgu_ln_b,
          w_spatial, b_spatial, ln1_g, ln1_b, w_peer_q, peer_sub_keys, peer_u, peer_v, ln2_g, ln2_b, out):
    with ExitStack() as ctx:
        def sb(name, shape, dt=F32):
            return ctx.enter_context(nc.sbuf_tensor(name, shape, dt))

        def sem(name):
            return ctx.enter_context(nc.semaphore(name))

        x_sb = sb("x_sb", [P, TILES, D])
        h_sb = sb("h_sb", [P, TILES, D])
        hT = sb("hT", [P, KC, SEQ])
        wpq = sb("wpq", [P, HEADS * KC * 256])
        small = sb("small", [P, 3 * 1024])
        cond = sb("cond", [P, 4, D])
        ln1 = sb("ln1", [P, 2, D])
        ln2 = sb("ln2", [P, 2, D])
        keysT = sb("keysT", [P, 2 * HEADS, NKEYS])
        ring = sb("ring", [P, ROWS * D])
        ident = sb("ident", [P, P])
        ones = sb("ones", [P, P])
        zero_tile = sb("zero_tile", [P, P])
        c_col = sb("c_col", [P, 3, KC])
        mod1 = sb("mod1", [P, 2, KC])
        stats = sb("stats", [P, 8, 2, 6])
        moments = sb("moments", [P, 8, 2])
        std = sb("std", [P, 8, 2])
        gst = sb("gst", [P, 4, 2 * HEADS])
        amax = sb("amax", [P, HEADS, 2])
        asum = sb("asum", [P, 2, HEADS, 2])
        eps = sb("eps", [P, 1])
        iota16 = sb("iota16", [P, TOPK])

        qT = wpq[:, 0:1024].rearrange("p (c t) -> p c t", c=WC)
        kT = wpq[:, 1024:2048].rearrange("p (c t) -> p c t", c=WC)
        v_sb = wpq[:, 2048:3072].rearrange("p (t n) -> p t n", t=TILES)
        negdist = wpq[:, 3072:3456]
        probs = wpq[:, 3456:4224].rearrange("p (a n) -> p a n", a=2)
        probsT = wpq[:, 4224:4992].rearrange("p (a n) -> p a n", a=2)
        spatT = wpq[:, 4992:6016].rearrange("p (g t) -> p g t", t=P)
        sgu_gb = wpq[:, 6016:7040].rearrange("p (a n) -> p a n", a=2)
        b_spat = wpq[:, 7040:7552].rearrange("p (c t) -> p c t", c=WC)
        iota_i = wpq[:, 7552:7952].bitcast(I32)
        EARLY = 6
        gates = wpq[:, 12288:16384]
        gates_v = gates.rearrange("p (t k a n) -> p t k a n", t=TILES, k=KC, a=2)
        b1 = wpq[0:2 * KC, 0:P]
        keys_nat = wpq[:, 8192:10240].rearrange("p (m d) -> p m d", d=NKEYS)
        cacc = ln2[:, 0, :].rearrange("p (a n) -> p a n", a=2)
        scratch = ln2[:, 1, :]
        uT = small[:, 0:1024].rearrange("p (c t) -> p c t", c=WC)
        gv_flat = small[:, 1024:2048]
        gv = gv_flat.rearrange("p (t n) -> p t n", t=TILES)
        gv_g = gv_flat.rearrange("p (g n) -> p g n", n=HD)
        attnT = small[:, 2048:3072].rearrange("p (c t) -> p c t", c=WC)
        spat_nat = small[:, 2048:3072].rearrange("p (g s) -> p g s", s=P)
        sc = small[:, 0:256]
        sr = small[:, 256:512]
        cand = small[:, 512:768]
        candr = small[:, 768:1024]
        onehot = small[:, 512:1024]
        q_tok = small[:, 1024:1280]
        qTs = small[:, 1280:1536].rearrange("p (c t) -> p c t", c=2)
        diag = small[:, 1536:2560].rearrange("p (e n) -> p e n", e=GROUP)
        top = small[:, 2560:2592]
        topi = small[:, 2592:2624].bitcast(U32)
        topf = small[:, 2624:2656]
        best = small[:, 2656:2672]
        pos = small[:, 2672:2688].bitcast(U32)
        hilo = small[:, 2688:2720].bitcast(U32)
        hilof = small[:, 2720:2752]
        sel = small[:, 2752:2784]
        nbest = small[:, 2784:2786]
        esum = small[:, 2786:2788]
        rsum = small[:, 2788:2790]
        expv = small[:, 2790:2822].rearrange("p (a k) -> p a k", a=2)
        acol = small[:, 2822:2838].rearrange("p (a k) -> p a k", a=2)
        gcol = small[:, 2838:2854].rearrange("p (a k) -> p a k", a=2)
        wts = small[:, 2854:2870].rearrange("p (a k) -> p a k", a=2)
        idx = small[:, 2870:2902].bitcast(U32)

        def row(first, e):
            r = (first + e) % ROWS
            return ring[:, r * D:(r + 1) * D]

        u_ring = [row(UROW, e) for e in range(GROUP)]
        v_ring = [row(VROW, e) for e in range(GROUP)]

        def slot(b):
            return ring[:, SLOT[b] * KC * BLK:(SLOT[b] + 1) * KC * BLK]

        bank = [ctx.enter_context(nc.psum_tensor(f"bank{i}", [P, BLK], F32)) for i in range(8)]
        PIECE_BANKS = (0, 1)
        SCORE_BANKS = (2, 3)
        TURN_BANK, GATE_BANK, ATTN_BANK, COND_BANK = 4, 5, 6, 7
        UP_BANKS = ((0, 1, 4, 5), (4, 5, 2, 3))
        OUT_BANKS = ((2, 3), (4, 5))
        XT_BANKS, HT_BANKS = (2, 3, 4, 5), (6, 7)
        WT_BANKS = (2, 3, 4, 5, 6, 2)
        Q_BANK, QT_BANK = 0, 1
        ACC_BANKS = ((2, 3), (4, 5))

        x_in = sem("x_in")
        c_in = sem("c_in")
        bcond_in = [sem(f"bcond_in{i}") for i in range(2)]
        keys_in = sem("keys_in")
        spat_in = sem("spat_in")
        sgu_in = sem("sgu_in")
        b_spat_in = sem("b_spat_in")
        w_arrived = [sem(f"w_arrived{i}") for i in range(SLOTS)]
        c_first = {n: sem(f"c{n}_first") for n in (2, 3)}
        in0_first = sem("in0_first")
        ln1_in = sem("ln1_in")
        ln2_in = sem("ln2_in")
        wpq_in = [sem(f"wpq_in{i}") for i in range(2)]
        u_in = [sem(f"u_in{i}") for i in range(GROUP)]
        v_in = [sem(f"v_in{i}") for i in range(GROUP)]
        out_stored = sem("out_stored")

        consts = sem("consts")
        spat_masked = sem("spat_masked")
        dve_step = sem("dve_step")
        topk_step = sem("topk_step")
        silu_tanh = sem("silu_tanh")
        var_ready = sem("var_ready")
        std_ready = sem("std_ready")
        xn_done = sem("xn_done")
        cacc_ready = sem("cacc_ready")
        cond_sum = sem("cond_sum")
        cond_saved = sem("cond_saved")
        xT_ready = sem("xT_ready")
        mod1_ready = sem("mod1_ready")
        wT_ready = sem("wT_ready")
        wT_saved = sem("wT_saved")
        hT_saved_act = sem("hT_saved_act")
        hT_saved_dve = sem("hT_saved_dve")
        h2T_ready = sem("h2T_ready")
        h2T_saved = sem("h2T_saved")
        piece_ready = sem("piece_ready")
        piece_saved = sem("piece_saved")
        gvar_ready = sem("gvar_ready")
        gstd_ready = sem("gstd_ready")
        vv_ready = sem("vv_ready")
        scores_ready = sem("scores_ready")
        max_ready = sem("max_ready")
        exp_done = sem("exp_done")
        probs_ready = sem("probs_ready")
        turned = sem("turned")
        turned_saved = sem("turned_saved")
        attn_ready = sem("attn_ready")
        attn_saved = sem("attn_saved")
        gate_ready = sem("gate_ready")
        gate_saved = sem("gate_saved")
        up_ready = sem("up_ready")
        merged = sem("merged")
        o_ready = sem("o_ready")
        acc_ready = sem("acc_ready")
        h2_ready = sem("h2_ready")
        q_ready = sem("q_ready")
        q_saved = sem("q_saved")
        qT_ready = sem("qT_ready")
        qT_saved = sem("qT_saved")
        s_ready = sem("s_ready")
        s_saved = sem("s_saved")
        best_ready = sem("best_ready")
        idx_ready = sem("idx_ready")
        wexp_done = sem("wexp_done")
        rsum_ready = sem("rsum_ready")
        dots_done = sem("dots_done")
        gelu_done = sem("gelu_done")
        wts_ready = sem("wts_ready")
        diag_ready = sem("diag_ready")
        v_used = sem("v_used")
        out_ready = sem("out_ready")
        pool_turn = sem("pool_turn")
        dve_turn = sem("dve_turn")

        def hold(engine, turn, s, value):
            engine.wait_ge(s, value)
            engine.sem_inc(turn, 1)

        block = ctx.enter_context(nc.Block())

        @block.sync
        def _(sp):
            w_of = {
                "c": w_cond[0].rearrange("(p k) n -> p k n", k=KC),
                "in": w_in[0].rearrange("(k p) n -> p k n", p=P),
                "o": w_out[0].rearrange("(k p) n -> p k n", p=P),
            }
            up_of = {"ua": w_attn_up[0].rearrange("(k p) n -> p k n", p=P),
                     "ug": w_gmlp_up[0].rearrange("(k p) n -> p k n", p=P)}

            sp.dma_start(x_sb[:], x[0].rearrange("(t p) d -> p t d", p=P)).then_inc(x_in, 16)
            for n, b in enumerate(STREAM):
                kind, i = b
                if n >= SLOTS:
                    old, j = STREAM[n - SLOTS]
                    if old == "c":
                        sp.wait_ge(cacc_ready, j + 1)
                        if j in TE_ROWS:
                            sp.wait_ge(cond_sum, j + 1)
                    elif old == "in":
                        sp.wait_ge(piece_ready, 2 * j + 2)
                    else:
                        sp.wait_ge(up_ready, KC)
                if kind in up_of:
                    sp.dma_start(slot(b).rearrange("p (k n) -> p k n", k=WC), up_of[kind]).then_inc(w_arrived[SLOT[b]], 16)
                else:
                    dst, src = slot(b).rearrange("p (k n) -> p k n", k=KC), w_of[kind][:, :, i * BLK:(i + 1) * BLK]
                    if b in (("c", 2), ("c", 3)):
                        sp.dma_start(dst[:, 0:KC // 2, :], src[:, 0:KC // 2, :]).then_inc(c_first[i], 16)
                        dst, src = dst[:, KC // 2:KC, :], src[:, KC // 2:KC, :]
                    if b == ("in", 0):
                        sp.dma_start(dst[:, :, 0:SEQ], src[:, :, 0:SEQ]).then_inc(in0_first, 16)
                        dst, src = dst[:, :, SEQ:BLK], src[:, :, SEQ:BLK]
                    sp.dma_start(dst, src).then_inc(w_arrived[SLOT[b]], 16)
                if b == ("c", 4):
                    sp.dma_start(cond[:].rearrange("p a n -> p (a n)"),
                                 b_cond[0:1, 2 * D:6 * D].broadcast_to([P, 4 * D])).then_inc(bcond_in[1], 16)
                if b == ("c", 10):
                    sp.dma_start(ln1[:, LN_G, :], ln1_g[0:1, :].broadcast_to([P, D])).then_inc(ln1_in, 16)
                    sp.dma_start(ln1[:, LN_B, :], ln1_b[0:1, :].broadcast_to([P, D])).then_inc(ln1_in, 16)
            wq_of = w_peer_q[0].rearrange("(k p) n -> p k n", p=P)
            for h in range(HEADS):
                if h == 0:
                    sp.wait_ge(attn_ready, HEADS)
                    sp.wait_ge(gate_saved, 2)
                if h >= EARLY:
                    sp.wait_ge(merged, 4 * (h - EARLY + 1))
                sp.dma_start(wpq[:, h * KC * 256:(h + 1) * KC * 256].rearrange("p (k n) -> p k n", k=KC),
                             wq_of[:, :, h * 256:(h + 1) * 256]).then_inc(wpq_in[int(h >= EARLY)], 16)
            sp.wait_ge(cond_sum, 12)
            sp.dma_start(ln2[:, LN_G, :], ln2_g[0:1, :].broadcast_to([P, D])).then_inc(ln2_in, 16)
            sp.dma_start(ln2[:, LN_B, :], ln2_b[0:1, :].broadcast_to([P, D])).then_inc(ln2_in, 16)
            for t in range(TILES):
                for i in range(2):
                    sp.wait_ge(out_ready, 2 * t + i + 1)
                    cols = slice(i * BLK, (i + 1) * BLK)
                    sp.dma_start(out[0, t * P:(t + 1) * P, cols], h_sb[:, t, cols]).then_inc(out_stored, 16)
            sp.wait_ge(out_stored, 16 * 2 * TILES)

        @block.gpsimd
        def _(pool):
            nc.gpsimd.memset(ones[:], 1.0).then_inc(consts, 1)
            nc.gpsimd.memset(eps[:], EPS).then_inc(consts, 1)
            nc.gpsimd.memset(ident[:], 0.0).then_inc(consts, 1)
            nc.gpsimd.memset(zero_tile[:], 0.0).then_inc(consts, 1)
            nc.gpsimd.iota(iota_i[:, 0:P], pattern=[[1, P]], base=0, channel_multiplier=-1).then_inc(consts, 1)
            nc.gpsimd.iota(iota_i[:, P:3 * P], pattern=[[1, 2 * P]], base=-P, channel_multiplier=-1).then_inc(consts, 1)
            nc.gpsimd.iota(iota_i[:, 3 * P:3 * P + TOPK], pattern=[[1, TOPK]], base=0, channel_multiplier=0).then_inc(consts, 1)
            pool.wait_ge(consts, 7)
            nc.gpsimd.affine_select(out=ident[:], in_=ident[:], compare_op=ALU.not_equal, fill=1.0, base=0,
                                    pattern=[[-1, P]], channel_multiplier=1).then_inc(consts, 1)
            nc.gpsimd.tensor_copy(negdist, iota_i[:, 0:3 * P]).then_inc(consts, 1)
            nc.gpsimd.tensor_copy(iota16[:], iota_i[:, 3 * P:3 * P + TOPK]).then_inc(consts, 1)
            pool.wait_ge(consts, 10)
            nc.gpsimd.affine_select(out=negdist[:, 0:P], in_=negdist[:, 0:P], compare_op=ALU.is_ge, fill=FAR, base=0,
                                    pattern=[[-1, P]], channel_multiplier=1).then_inc(consts, 1)
            nc.gpsimd.affine_select(out=negdist[:, P:3 * P], in_=negdist[:, P:3 * P], compare_op=ALU.is_ge, fill=FAR,
                                    base=P, pattern=[[-1, 2 * P]], channel_multiplier=1).then_inc(consts, 1)
            pool.wait_ge(spat_in, 16)
            nc.gpsimd.affine_select(out=spat_nat, in_=spat_nat, compare_op=ALU.is_ge, fill=0.0, base=0,
                                    pattern=[[0, HEADS], [-1, P]], channel_multiplier=1).then_inc(spat_masked, 1)

            def gather_pair(i, a):
                p = 2 * i + a

                def gather(table, dst, e, k, landed):
                    nc.gpsimd.indirect_dma_start(
                        out=dst[e], out_offset=None, in_=table[0],
                        in_offset=bass.IndirectOffsetOnAxis(ap=idx[:, k:k + 1], axis=0)).then_inc(landed[e], 16)

                hold(pool, pool_turn, idx_ready, p + 1)
                for g in range(2):
                    n = 2 * p + g
                    first = a * TOPK + g * GROUP
                    hold(pool, pool_turn, dots_done, GROUP * n + GROUP)
                    for e in range(GROUP):
                        gather(peer_u, u_ring, e, first + e, u_in)
                    for e in range(GROUP):
                        if e % 2 == 0:
                            hold(pool, pool_turn, v_used, GROUP * n + e + 2)
                        gather(peer_v, v_ring, e, first + e, v_in)

            with pool.Fori(0, PAIRS // 2) as i:
                gather_pair(i, 0)
                gather_pair(i, 1)

        @block.scalar
        def _(act):
            act.dma_start(c_col[:, 0, :], c[0].rearrange("(p k) -> p k", k=KC)).then_inc(c_in, 16)
            act.dma_start(b1, b_cond[0, 0:2 * D].rearrange("(k n) -> k n", n=P)).then_inc(bcond_in[0], 16)
            act.wait_ge(c_in, 16)
            nc.scalar.activation(c_col[:, 1, :], c_col[:, 0, :], ACT.Tanh, scale=0.5).then_inc(silu_tanh, 1)

            def root(n):
                act.wait_ge(var_ready, n + 1)
                nc.scalar.activation(std[:, n, 0:1], moments[:, n, 1:2], ACT.Sqrt, bias=eps[:]).then_inc(std_ready, 1)

            act.wait_ge(consts, 2)
            root(0)
            root(1)

            def save_wT(n):
                act.wait_ge(wT_ready, n + 1)
                dst = spatT[:, 4 * n:4 * n + 4, :] if n < 2 else keysT[:, 4 * n - 8:4 * n - 4, :]
                nc.scalar.activation(dst.rearrange("p g t -> p (g t)"), bank[WT_BANKS[n]][:], ACT.Copy).then_inc(wT_saved, 1)

            act.wait_ge(xT_ready, 1)
            act.wait_ge(mod1_ready, 2)
            for r in (0, 2):
                for m in range(2):
                    k = 2 * r + m
                    nc.scalar.activation(hT[:, k, :], bank[XT_BANKS[r]][:, m * SEQ:(m + 1) * SEQ], ACT.Identity,
                                         scale=mod1[:, 1, k:k + 1], bias=mod1[:, 0, k:k + 1]).then_inc(hT_saved_act, 1)

            act.dma_start(spat_nat, w_spatial[0].rearrange("g t s -> t g s")).then_inc(spat_in, 16)
            act.dma_start(keys_nat, peer_sub_keys[0].rearrange("h c n d -> n (h c) d")).then_inc(keys_in, 16)
            for i in range(2):
                act.dma_start(b_spat[i * HD:(i + 1) * HD, :, :], b_spatial[0].rearrange("(c a) t -> a c t", a=2)[i:i + 1]
                              .broadcast_to([HD, WC, P])).then_inc(b_spat_in, 16)
            for i, v in enumerate((sgu_ln_g, sgu_ln_b)):
                act.dma_start(sgu_gb[:, i, :], v[0:1].rearrange("a g d -> a (g d)").broadcast_to([P, WIDTH])).then_inc(sgu_in, 16)

            def save_h2T(t):
                act.wait_ge(h2T_ready, t + 1)
                for r in range(2):
                    nc.scalar.activation(hT[:, 4 * r:4 * r + 4, t * P:(t + 1) * P],
                                         bank[HT_BANKS[r]][:].rearrange("p (k n) -> p k n", n=P), ACT.Copy).then_inc(h2T_saved, 1)

            def piece(n):
                b, half = n // 2, n % 2
                act.wait_ge(piece_ready, n + 1)
                src = bank[PIECE_BANKS[n % 2]][:]
                two = slice(2 * half, 2 * half + 2)
                if b == IN_Q:
                    ins = nc.scalar.activation(qT[:, two, :].rearrange("p c t -> p (c t)"), src, ACT.Copy, scale=HD ** -0.5)
                elif b == IN_K:
                    ins = nc.scalar.activation(kT[:, two, :].rearrange("p c t -> p (c t)"), src, ACT.Copy)
                elif b == IN_V:
                    ins = nc.scalar.activation(v_sb[:, half, :], src, ACT.Copy)
                elif b == IN_GU:
                    ins = nc.scalar.activation(uT[:, two, :].rearrange("p c t -> p (c t)"), src, ACT.Gelu)
                elif b == IN_GV:
                    ins = nc.scalar.activation(gv[:, half, :], src, ACT.Gelu)
                else:
                    which = int(b >= IN_GG)
                    first = 4 * (b - (IN_GG if which else IN_GA)) + 2 * half
                    ins = nc.scalar.activation(gates_v[:, :, first:first + 2, which, :],
                                               src.rearrange("p (c t n) -> p t c n", c=2, t=TILES), ACT.Tanh, scale=0.5)
                ins.then_inc(piece_saved, 1)

            for n in range(2 * IN_GA):
                piece(n)
                if n == 3:
                    save_wT(0)
                    save_wT(1)
                if n == 5:
                    for m in range(2, 6):
                        save_wT(m)
            act.wait_ge(gvar_ready, 1)
            nc.scalar.activation(gst[:, 2, :], gst[:, 1, :], ACT.Sqrt, bias=eps[:], scale=1.0 / HD).then_inc(gstd_ready, 1)

            for j in range(HEADS + 2):
                if j < HEADS:
                    for t in range(TILES):
                        act.wait_ge(max_ready, 2 * j + t + 1)
                        cols = slice(0, P) if t == 0 else slice(P, 3 * P)
                        nc.scalar.activation(probs[:, j % 2, cols], probs[:, j % 2, cols], ACT.Exp, bias=amax[:, j, t:t + 1],
                                             accum_out=asum[:, 0, j, t:t + 1]).then_inc(exp_done, 1)
                    if j < HEADS - 1:
                        piece(2 * IN_GA + j)
                if 1 <= j <= HEADS:
                    act.wait_ge(turned, j)
                    if j >= 3:
                        act.wait_ge(attn_ready, j - 2)
                    nc.scalar.activation(probsT[:, (j - 1) % 2, :], bank[TURN_BANK][:, 0:3 * P], ACT.Copy).then_inc(turned_saved, 1)
                if j == HEADS:
                    piece(PIECES - 1)
                if j >= 3 and j % 2 == 1:
                    m = (j - 3) // 2
                    act.wait_ge(attn_ready, 2 * m + 2)
                    nc.scalar.activation(attnT[:, m, :], bank[ATTN_BANK][:, (m % 2) * SEQ:(m % 2 + 1) * SEQ],
                                         ACT.Copy).then_inc(attn_saved, 1)

            def save_scores(p):
                if not (isinstance(p, int) and p == 0):
                    act.wait_ge(q_ready, p)
                    nc.scalar.activation(q_tok, bank[Q_BANK][:, 0:256], ACT.Copy).then_inc(q_saved, 1)
                act.wait_ge(qT_ready, p + 1)
                nc.scalar.activation(qTs.rearrange("p c t -> p (c t)"), bank[QT_BANK][:, 0:256], ACT.Copy).then_inc(qT_saved, 1)
                act.wait_ge(s_ready, p + 1)
                nc.scalar.activation(sc, bank[QT_BANK][:, 256:512], ACT.Copy).then_inc(s_saved, 1)

            def softmax_exp(p, a):
                act.wait_ge(best_ready, p + 1)
                nc.scalar.activation(expv[:, a, :], best, ACT.Exp, bias=nbest[:, a:a + 1],
                                     accum_out=esum[:, a:a + 1]).then_inc(wexp_done, 1)

            def weigh(i, a, following=True):
                p = 2 * i + a
                if following:
                    save_scores(p + 1)
                for g in range(2):
                    n = 2 * p + g
                    act.wait_ge(dots_done, GROUP * n + 2 * GROUP)
                    nc.scalar.activation(gcol[:, g, :], acol[:, g, :], ACT.Gelu).then_inc(gelu_done, 1)
                    act.wait_ge(wts_ready, n + 1)
                    for e in PE_ROWS if (following, g) == (False, 1) else range(GROUP):
                        if e % 2 == 0:
                            act.wait_ge(v_used, GROUP * n + e + 2)
                        nc.scalar.activation(diag[:, e, :], ident[:], ACT.Copy, scale=wts[:, g, e:e + 1]).then_inc(diag_ready, 1)
                    if g == 0 and following:
                        softmax_exp(p + 1, 1 - a)

            root(2)
            root(3)
            save_h2T(0)
            save_scores(0)
            softmax_exp(0, 0)
            weigh(0, 0)
            root(4)
            root(5)
            weigh(0, 1)
            save_h2T(1)
            with act.Fori(1, PAIRS // 2 - 1) as i:
                weigh(i, 0)
                weigh(i, 1)
            root(6)
            weigh(PAIRS // 2 - 1, 0)
            weigh(PAIRS // 2 - 1, 1, following=False)
            root(7)

        @block.vector
        def _(dve):
            steps = [0]

            def link(ins):
                steps[0] += 1
                ins.then_inc(dve_step, 1)
                dve.wait_ge(dve_step, steps[0])

            V = nc.vector

            def variance(n, src):
                for i in range(2):
                    last = V.bn_stats(stats[:, n, i, :], src[:, i * BLK:(i + 1) * BLK])
                    if i == 0:
                        last.then_inc(dve_step, 1)
                        steps[0] += 1
                link(last)
                V.bn_aggr(moments[:, n, :], stats[:, n, :, :].rearrange("p a b -> p (a b)")).then_inc(var_ready, 1)

            def normalise(n, dst, src):
                dve.wait_ge(std_ready, n + 1)
                link(V.reciprocal(std[:, n, 1:2], std[:, n, 0:1]))
                return V.tensor_scalar(dst, src, moments[:, n, 0:1], std[:, n, 1:2], ALU.subtract, ALU.mult)

            dve.wait_ge(x_in, 16)
            for t in range(TILES):
                variance(t, x_sb[:, t, :])
            dve.wait_ge(silu_tanh, 1)
            link(V.scalar_tensor_tensor(out=c_col[:, 2, :], in0=c_col[:, 1, :], scalar=1.0, in1=c_col[:, 0, :],
                                        op0=ALU.add, op1=ALU.mult))
            link(V.tensor_scalar(c_col[:, 2, :], c_col[:, 2, :], 0.5, None, ALU.mult))
            for t in range(TILES):
                normalise(t, h_sb[:, t, :], x_sb[:, t, :]).then_inc(xn_done, 1)

            def cond_block(n):
                b = ("c", n)
                if n in c_first:
                    dve.wait_ge(c_first[n], 16)
                else:
                    dve.wait_ge(w_arrived[SLOT[b]], 16 * (TURN[b] + 1))
                if n >= 2:
                    dve.wait_ge(cond_sum, n - 1)
                w = slot(b).rearrange("p (k n) -> p k n", k=KC)
                acc = cacc[:, n % 2, :]
                link(V.tensor_scalar(acc, w[:, 0, :], c_col[:, 2, 0:1], None, ALU.mult))
                last_row = KC - 1 - TE_ROWS.get(n, 0)
                for k in range(1, last_row + 1):
                    if n in c_first and k == KC // 2:
                        dve.wait_ge(w_arrived[SLOT[b]], 16)
                    ins = V.scalar_tensor_tensor(out=acc, in0=w[:, k, :], scalar=c_col[:, 2, k:k + 1], in1=acc,
                                                 op0=ALU.mult, op1=ALU.add)
                    if k < last_row:
                        link(ins)
                ins.then_inc(cacc_ready, 1)

            def cond_save(n):
                dve.wait_ge(cond_sum, n + 1)
                if n == 4:
                    dve.wait_ge(bcond_in[1], 16)
                row = n // 2 - 2
                part = cond[:, row, (n % 2) * BLK:(n % 2 + 1) * BLK]
                one = 0.0 if row == SH2 else 1.0
                V.scalar_tensor_tensor(out=part, in0=bank[COND_BANK][:], scalar=one, in1=part,
                                       op0=ALU.add, op1=ALU.add).then_inc(cond_saved, 1)

            for n in range(4):
                cond_block(n)
            dve.wait_ge(cond_sum, 4)
            V.tensor_copy(mod1[:, 0, :], bank[COND_BANK][:, 0:KC]).then_inc(mod1_ready, 1)
            V.tensor_scalar(mod1[:, 1, :], bank[COND_BANK][:, KC:2 * KC], 1.0, None, ALU.add).then_inc(mod1_ready, 1)
            dve.wait_ge(mod1_ready, 2)
            dve.wait_ge(xT_ready, 1)
            for r in (1, 3):
                for m in range(2):
                    k = 2 * r + m
                    V.tensor_scalar(hT[:, k, :], bank[XT_BANKS[r]][:, m * SEQ:(m + 1) * SEQ], mod1[:, 1, k:k + 1],
                                    mod1[:, 0, k:k + 1], ALU.mult, ALU.add).then_inc(hT_saved_dve, 1)

            for n in range(4, 9):
                cond_block(n)
                if n > 4:
                    cond_save(n - 1)
            cond_save(8)

            def wide(v):
                return v.unsqueeze(2).broadcast_to([P, 2 * HEADS, HD])

            sq = scratch.rearrange("p (g n) -> p g n", n=HD)
            dve.wait_ge(piece_saved, 2 * IN_GV + 2)
            link(V.tensor_reduce(gst[:, 0, :], gv_g, AX_X, ALU.add))
            link(V.tensor_scalar(gst[:, 0, :], gst[:, 0, :], 1.0 / HD, None, ALU.mult))
            link(V.tensor_tensor(gv_g, gv_g, wide(gst[:, 0, :]), ALU.subtract))
            link(V.tensor_tensor(sq, gv_g, gv_g, ALU.mult))
            V.tensor_reduce(gst[:, 1, :], sq, AX_X, ALU.add).then_inc(gvar_ready, 1)
            dve.wait_ge(gstd_ready, 1)
            link(V.reciprocal(gst[:, 3, :], gst[:, 2, :]))
            link(V.tensor_tensor(gv_g, gv_g, wide(gst[:, 3, :]), ALU.mult))
            dve.wait_ge(sgu_in, 32)
            for i, op in ((0, ALU.mult), (1, ALU.add)):
                ins = V.tensor_tensor(gv, gv, sgu_gb[:, i, :].unsqueeze(1).broadcast_to([P, TILES, WIDTH]), op)
                if i == 0:
                    link(ins)
            ins.then_inc(vv_ready, 1)

            def save_gate(r):
                dve.wait_ge(gate_ready, r + 1)
                if r == 0:
                    dve.wait_ge(b_spat_in, 32)
                else:
                    dve.wait_ge(gate_saved, r)
                part = uT[:, 2 * r:2 * r + 2, :].rearrange("p c t -> p (c t)")
                gate = scratch[:, 0:BLK]
                link(V.tensor_tensor(gate.rearrange("p (c t n) -> p c t n", c=2, t=TILES),
                                     bank[GATE_BANK][:].rearrange("p (c t n) -> p c t n", c=2, t=TILES),
                                     b_spat[:, 2 * r:2 * r + 2, :].unsqueeze(2).broadcast_to([P, 2, TILES, P]), ALU.add))
                V.tensor_tensor(part, part, gate, ALU.mult).then_inc(gate_saved, 1)

            dve.wait_ge(consts, 12)
            for j in range(HEADS):
                pj = probs[:, j % 2, :]
                if j >= 2:
                    dve.wait_ge(turned, j - 1)
                dve.wait_ge(scores_ready, j + 1)
                link(V.scalar_tensor_tensor(out=pj, in0=negdist, scalar=2.0 ** -(j + 1), in1=bank[SCORE_BANKS[j % 2]][:, 0:3 * P],
                                            op0=ALU.mult, op1=ALU.add))
                for t in range(TILES):
                    cols = slice(0, P) if t == 0 else slice(P, 3 * P)
                    V.tensor_reduce(amax[:, j, t:t + 1], pj[:, cols], AX_X, ALU.max, negate=True).then_inc(max_ready, 1)
                dve.wait_ge(exp_done, 2 * j + 2)
                link(V.reciprocal(asum[:, 1, j, :], asum[:, 0, j, :]))
                for t in range(TILES):
                    cols = slice(0, P) if t == 0 else slice(P, 3 * P)
                    V.tensor_scalar(pj[:, cols], pj[:, cols], asum[:, 1, j, t:t + 1], None, ALU.mult).then_inc(probs_ready, 1)
                if j in (0, 2, 4):
                    cond_block(9 + j // 2)
                if j in (3, 5, 7):
                    cond_save(8 + j // 2)
                if j == 5:
                    save_gate(0)
            save_gate(1)

            def merge(t):
                tmp = scratch[:, 0:BLK]
                for r in range(KC // 2):
                    n = (KC // 2) * t + r
                    dve.wait_ge(up_ready, n + 1)
                    if n:
                        dve.wait_ge(merged, n)
                    g0 = (t * KC + 2 * r) * 2 * P
                    link(V.scalar_tensor_tensor(out=tmp, in0=gates[:, g0:g0 + BLK], scalar=1.0, in1=bank[UP_BANKS[t][r]][:],
                                                op0=ALU.add, op1=ALU.mult))
                    halves = tmp.rearrange("p (k a n) -> p k a n", k=2, a=2)
                    V.tensor_tensor(hT[:, 2 * r:2 * r + 2, t * P:(t + 1) * P], halves[:, :, 0, :], halves[:, :, 1, :],
                                    ALU.add).then_inc(merged, 1)

            dve.wait_ge(piece_saved, PIECES)
            merge(0)

            def residual(n, t, banks, gate, halve, dst, ready, counts, base=None):
                for i in range(2):
                    cols = slice(i * BLK, (i + 1) * BLK)
                    dve.wait_ge(ready, counts[i])
                    link(V.scalar_tensor_tensor(out=dst[:, cols], in0=bank[banks[i]][:], scalar=halve,
                                                in1=cond[:, gate, cols], op0=ALU.mult, op1=ALU.mult))
                    if base is None:
                        link(V.scalar_tensor_tensor(out=dst[:, cols], in0=x_sb[:, t, cols], scalar=ALPHA,
                                                    in1=dst[:, cols], op0=ALU.mult, op1=ALU.add))
                    else:
                        link(V.tensor_tensor(dst[:, cols], dst[:, cols], base[:, cols], ALU.add))
                    link(V.bn_stats(stats[:, n, i, :], dst[:, cols]))
                V.bn_aggr(moments[:, n, :], stats[:, n, :, :].rearrange("p a b -> p (a b)")).then_inc(var_ready, 1)

            def centre(n, dst, src, g):
                dve.wait_ge(var_ready, n + 1)
                link(V.scalar_tensor_tensor(out=dst, in0=src, scalar=moments[:, n, 0:1], in1=g,
                                            op0=ALU.subtract, op1=ALU.mult))
                dve.wait_ge(std_ready, n + 1)
                link(V.reciprocal(std[:, n, 1:2], std[:, n, 0:1]))

            def scale_shift(n, dst, src, b, i):
                cols = slice(i * BLK, (i + 1) * BLK)
                return V.scalar_tensor_tensor(out=dst[:, cols], in0=src[:, cols], scalar=std[:, n, 1:2], in1=b[:, cols],
                                              op0=ALU.mult, op1=ALU.add)

            TOPK_STEPS = 23

            class Steps:

                def __init__(self, p, n):
                    self.p, self.n = p, n

                def __call__(self, *many):
                    for ins in many:
                        self.n += 1
                        ins.then_inc(topk_step, 1)
                    hold(dve, dve_turn, topk_step, self.p * TOPK_STEPS + self.n)

            HALF_STEPS = 11

            def topk_halves(p):
                step = Steps(p, 0)
                hold(dve, dve_turn, s_saved, p + 1)
                half = [slice(0, NKEYS), slice(NKEYS, 2 * NKEYS)]
                hi8 = [slice(0, 8), slice(TOPK, TOPK + 8)]
                lo8 = [slice(8, TOPK), slice(TOPK + 8, 2 * TOPK)]
                step(*[V.max(top[:, hi8[c]], sc[:, half[c]]) for c in range(2)])
                step(*[V.match_replace(sr[:, half[c]], top[:, hi8[c]], sc[:, half[c]], LOWEST) for c in range(2)],
                     *[V.max_index(topi[:, hi8[c]], top[:, hi8[c]], sc[:, half[c]]) for c in range(2)])
                step(*[V.max(top[:, lo8[c]], sr[:, half[c]]) for c in range(2)])
                step(*[V.max_index(topi[:, lo8[c]], top[:, lo8[c]], sr[:, half[c]]) for c in range(2)],
                     V.tensor_tensor(cand.rearrange("p (i j) -> p i j", i=TOPK),
                                     top[:, 0:TOPK].unsqueeze(2).broadcast_to([P, TOPK, TOPK]),
                                     top[:, TOPK:2 * TOPK].unsqueeze(1).broadcast_to([P, TOPK, TOPK]), ALU.add))
                assert step.n == HALF_STEPS, step.n

            def topk_sums(p, a):
                step = Steps(p, HALF_STEPS)
                step(V.max(best[:, 0:8], cand))
                step(V.match_replace(candr, best[:, 0:8], cand, LOWEST),
                     V.max_index(pos[:, 0:8], best[:, 0:8], cand),
                     V.tensor_scalar(nbest[:, a:a + 1], best[:, 0:1], -1.0, None, ALU.mult))
                V.max(best[:, 8:TOPK], candr).then_inc(best_ready, 1)
                hold(dve, dve_turn, best_ready, p + 1)
                step(V.max_index(pos[:, 8:TOPK], best[:, 8:TOPK], candr),
                     V.tensor_copy(topf, topi))
                step(V.tensor_scalar(hilo[:, 0:TOPK], pos, SHIFT, None, ALU.logical_shift_right),
                     V.tensor_scalar(hilo[:, TOPK:2 * TOPK], pos, MASK, None, ALU.bitwise_and))
                step(V.tensor_copy(hilof, hilo))
                oh = onehot.rearrange("p (m i) -> p m i", i=TOPK)
                oh4 = onehot.rearrange("p (c k i) -> p c k i", c=2, k=TOPK)
                step(V.tensor_tensor(oh, hilof.unsqueeze(2).broadcast_to([P, 2 * TOPK, TOPK]),
                                     iota16[:].unsqueeze(1).broadcast_to([P, 2 * TOPK, TOPK]), ALU.is_equal))
                step(V.tensor_tensor(oh4, oh4, topf.rearrange("p (c i) -> p c i", c=2).unsqueeze(2)
                                     .broadcast_to([P, 2, TOPK, TOPK]), ALU.mult))
                step(V.tensor_reduce(sel, oh, AX_X, ALU.add))
                assert step.n == TOPK_STEPS, step.n
                if not (isinstance(p, int) and p == 0):
                    hold(dve, dve_turn, v_used, p * TOPK - TOPK + GROUP)
                V.scalar_tensor_tensor(out=idx[:, a * TOPK:(a + 1) * TOPK], in0=sel[:, 0:TOPK], scalar=float(NKEYS),
                                       in1=sel[:, TOPK:2 * TOPK], op0=ALU.mult, op1=ALU.add).then_inc(idx_ready, 1)

            def weights(p, a, g):
                if g == 0:
                    dve.wait_ge(wexp_done, p + 1)
                    V.reciprocal(rsum[:, a:a + 1], esum[:, a:a + 1]).then_inc(rsum_ready, 1)
                dve.wait_ge(rsum_ready, p + 1)
                dve.wait_ge(gelu_done, 2 * p + g + 1)
                V.scalar_tensor_tensor(out=wts[:, g, :], in0=gcol[:, g, :], scalar=rsum[:, a:a + 1],
                                       in1=expv[:, a, g * GROUP:(g + 1) * GROUP], op0=ALU.mult, op1=ALU.mult).then_inc(wts_ready, 1)

            def dots(i, a, t, following=True):
                p = 2 * i + a
                for g in range(2):
                    for e in range(GROUP):
                        dve.wait_ge(u_in[e], 16 * (2 * p + g + 1))
                        V.tensor_tensor_reduce(u_ring[e], u_ring[e], h_sb[:, t, :], 1.0, 0.0, ALU.mult, ALU.add,
                                               acol[:, g, e:e + 1]).then_inc(dots_done, 1)
                    if g == 0 and following:
                        topk_halves(p + 1)
                    weights(p, a, g)
                    if g == 0 and following:
                        topk_sums(p + 1, 1 - a)

            def norm_and_modulate(t):
                n = 2 + 2 * t
                ht, xt = h_sb[:, t, :], x_sb[:, t, :]
                residual(n, t, OUT_BANKS[t], GT1, 0.5, ht, o_ready, (2 * t + 1, 2 * t + 2))
                centre(n, ht, ht, ln1[:, LN_G, :])
                for i in range(2):
                    link(scale_shift(n, xt, ht, ln1[:, LN_B, :], i))
                    link(V.bn_stats(stats[:, n + 1, i, :], xt[:, i * BLK:(i + 1) * BLK]))
                V.bn_aggr(moments[:, n + 1, :], stats[:, n + 1, :, :].rearrange("p a b -> p (a b)")).then_inc(var_ready, 1)
                centre(n + 1, ht, xt, cond[:, SC2, :])
                for i in range(2):
                    scale_shift(n + 1, ht, ht, cond[:, SH2, :], i).then_inc(h2_ready, 1)

            def own_rows():
                n, t = 2 * PAIRS - 1, TILES - 1
                base = u_ring[0]
                dve.wait_ge(wts_ready, n + 1)
                dve.wait_ge(dots_done, GROUP * (n + 2))
                for e in DVE_ROWS:
                    dve.wait_ge(v_in[e], 16 * (n + 1))
                    if e == DVE_ROWS[0]:
                        link(V.tensor_scalar(base, v_ring[e], wts[:, 1, e:e + 1], None, ALU.mult))
                    else:
                        link(V.scalar_tensor_tensor(out=base, in0=v_ring[e], scalar=wts[:, 1, e:e + 1], in1=base,
                                                    op0=ALU.mult, op1=ALU.add))
                link(V.tensor_tensor(base, base, cond[:, GT2, :], ALU.mult))
                link(V.scalar_tensor_tensor(out=base, in0=x_sb[:, t, :], scalar=ALPHA, in1=base, op0=ALU.mult, op1=ALU.add))
                return base

            def finish(t, base=None):
                n, ht = 6 + t, h_sb[:, t, :]
                if t == 0:
                    all_rows = GROUP + HEADS * TOPK
                    residual(n, t, ACC_BANKS[t], GT2, 1.0, ht, v_used, (all_rows, all_rows))
                else:
                    residual(n, t, ACC_BANKS[t], GT2, 1.0, ht, acc_ready, (1, 2), base)
                centre(n, ht, ht, ln2[:, LN_G, :])
                for i in range(2):
                    scale_shift(n, ht, ht, ln2[:, LN_B, :], i).then_inc(out_ready, 1)

            dve.wait_ge(ln1_in, 32)
            dve.wait_ge(cond_saved, 8)
            norm_and_modulate(0)
            dve.wait_ge(h2_ready, 2)
            merge(1)
            dve.sem_inc(dots_done, GROUP)
            topk_halves(0)
            topk_sums(0, 0)
            dots(0, 0, 0)
            norm_and_modulate(1)
            dots(0, 1, 0)
            with dve.Fori(1, HEADS // 2) as i:
                dots(i, 0, 0)
                dots(i, 1, 0)
            dve.wait_ge(h2_ready, 2 * TILES)
            with dve.Fori(HEADS // 2, PAIRS // 2 - 1) as i:
                dots(i, 0, 1)
                dots(i, 1, 1)
            dve.wait_ge(ln2_in, 32)
            finish(0)
            dots(PAIRS // 2 - 1, 0, 1)
            dots(PAIRS // 2 - 1, 1, 1, following=False)
            finish(1, own_rows())

        @block.tensor
        def _(pe):
            T = nc.tensor
            pe.wait_ge(consts, 8)

            for t in range(TILES):
                pe.wait_ge(xn_done, t + 1)
                for k in range(KC):
                    last = T.transpose(bank[XT_BANKS[k // 2]][:, k % 2 * SEQ + t * P:k % 2 * SEQ + (t + 1) * P],
                                       h_sb[:, t, k * P:(k + 1) * P], ident[:])
            last.then_inc(xT_ready, 1)

            pe.wait_ge(bcond_in[0], 16)
            T.matmul(bank[COND_BANK][:, 0:2 * KC], b1, ident[0:2 * KC, 0:2 * KC], start=True, stop=False, skip_group_check=True)

            def cond_columns(n):
                b = ("c", n)
                w = slot(b).rearrange("p (k n) -> p k n", k=KC)
                pe.wait_ge(w_arrived[SLOT[b]], 16)
                for m in range(BLK // P):
                    k = n * (BLK // P) + m
                    for row in range(KC - TE_ROWS[n], KC):
                        T.matmul(bank[COND_BANK][:, k:k + 1], w[:, row, m * P:(m + 1) * P], c_col[:, 2, row:row + 1],
                                 start=False, stop=False, skip_group_check=True)
                pe.wait_ge(cacc_ready, n + 1)
                for m in range(BLK // P):
                    k = n * (BLK // P) + m
                    last = T.matmul(bank[COND_BANK][:, k:k + 1], cacc[:, n % 2, m * P:(m + 1) * P], ones[:, 0:1],
                                    start=False, stop=True, skip_group_check=True)
                last.then_inc(cond_sum, 1)

            for n in range(4):
                cond_columns(n)

            def cond_total(n):
                pe.wait_ge(cacc_ready, n + 1)
                if n > 4:
                    pe.wait_ge(cond_saved, n - 4)
                T.matmul(bank[COND_BANK][:], ones[:], cacc[:, n % 2, :], start=True, stop=True).then_inc(cond_sum, 1)

            def turn_weights(n):
                if n == 5:
                    pe.wait_ge(wT_saved, 1)
                for g in range(4):
                    src = spat_nat[:, 4 * n + g, :] if n < 2 else keys_nat[:, 4 * n - 8 + g, :]
                    last = T.transpose(bank[WT_BANKS[n]][:, g * P:(g + 1) * P], src, ident[:])
                last.then_inc(wT_ready, 1)

            def arrived(b):
                pe.wait_ge(w_arrived[SLOT[b]], 16 * (TURN[b] + 1))

            def piece(n, parts=(0, 1)):
                b, half = n // 2, n % 2
                w = slot(("in", b)).rearrange("p (k n) -> p k n", k=KC)
                if n == 0:
                    pe.wait_ge(in0_first, 16)
                elif half == 0 or n == 1:
                    arrived(("in", b))
                if n >= 2 and 0 in parts:
                    pe.wait_ge(piece_saved, n - 1)
                dst = bank[PIECE_BANKS[n % 2]]
                if b in (IN_V, IN_GV):
                    for k in range(KC):
                        last = T.matmul(dst[:], hT[:, k, half * P:(half + 1) * P], w[:, k, :], start=(k == 0), stop=(k == KC - 1))
                else:
                    for m in parts:
                        col = (2 * half + m) * P
                        for i, k in enumerate(HT_ORDER):
                            if (n, m) == (0, 0):
                                pe.wait_ge(hT_saved_dve if k // 2 % 2 else hT_saved_act, i // 2 + 1)
                            last = T.matmul(dst[:, m * SEQ:(m + 1) * SEQ], w[:, k, col:col + P], hT[:, k, :],
                                            start=(i == 0), stop=(i == KC - 1))
                if 1 in parts:
                    last.then_inc(piece_ready, 1)

            HT_ORDER = (0, 2, 1, 3, 4, 6, 5, 7)
            for b in range(IN_GA):
                piece(2 * b)
                piece(2 * b + 1)
                if b == 1:
                    pe.wait_ge(spat_masked, 1)
                    turn_weights(0)
                    turn_weights(1)
                if b == 2:
                    pe.wait_ge(keys_in, 16)
                    for n in range(2, 6):
                        turn_weights(n)
                if b:
                    cond_total(3 + b)
            cond_total(3 + IN_GA)

            def scores(j):
                rows = slice(HD * (j % 2), HD * (j % 2) + HD)
                if j == 0:
                    pe.wait_ge(wT_saved, 6)
                if j >= 2:
                    pe.wait_ge(max_ready, 2 * j - 2)
                dst = bank[SCORE_BANKS[j % 2]]
                T.matmul(dst[:, 0:P], qT[rows, j // 2, 0:P], kT[rows, j // 2, 0:P], start=True, stop=True)
                T.matmul(dst[:, P:3 * P], qT[rows, j // 2, P:SEQ], kT[rows, j // 2, :], start=True, stop=True).then_inc(scores_ready, 1)

            def turn(j):
                pe.wait_ge(probs_ready, 2 * j + 2)
                if j:
                    pe.wait_ge(turned_saved, j)
                for m in range(3):
                    last = T.transpose(bank[TURN_BANK][:, m * P:(m + 1) * P], probs[:, j % 2, m * P:(m + 1) * P], ident[:])
                last.then_inc(turned, 1)

            def attend(j):
                pe.wait_ge(turned_saved, j + 1)
                if j % 2 == 0 and j >= 2:
                    pe.wait_ge(attn_saved, j // 2)
                rows = slice(HD * (j % 2), HD * (j % 2) + HD)
                col = (j // 2 % 2) * SEQ
                dst = bank[ATTN_BANK]
                vh = [v_sb[:, t, j * HD:(j + 1) * HD] for t in range(TILES)]
                pt = probsT[:, j % 2, :]
                T.matmul(dst[rows, col:col + P], vh[0], pt[:, 0:P], start=True, stop=True)
                T.matmul(dst[rows, col + P:col + SEQ], vh[0], pt[:, P:2 * P], start=True, stop=False)
                T.matmul(dst[rows, col + P:col + SEQ], vh[1], pt[:, 2 * P:3 * P], start=False, stop=True).then_inc(attn_ready, 1)

            def spatial(r):
                if r == 0:
                    pe.wait_ge(vv_ready, 1)
                else:
                    pe.wait_ge(gate_saved, r)
                for g in range(4 * r, 4 * r + 4):
                    rows = slice(HD * (g % 2), HD * (g % 2) + HD)
                    for t in range(TILES):
                        col = (g // 2 % 2) * SEQ + t * P
                        dst = bank[GATE_BANK][rows, col:col + P]
                        last = T.matmul(dst, gv[:, t, g * HD:(g + 1) * HD], spatT[:, g, :], start=True, stop=True)
                last.then_inc(gate_ready, 1)

            for j in range(HEADS + 2):
                if j < HEADS:
                    scores(j)
                    piece(2 * IN_GA + j, parts=(0,) if j == HEADS - 1 else (0, 1))
                if 1 <= j <= HEADS:
                    turn(j - 1)
                if j >= 2:
                    attend(j - 2)
                if j == HEADS:
                    piece(PIECES - 1, parts=(1,))
                if j in (2, 4, 6):
                    cond_total(8 + j // 2)
                if j in (4, 6):
                    spatial(j // 2 - 2)

            ups = [(slot((kind, 0)).rearrange("p (k n) -> p k n", k=WC), src) for kind, src in (("ua", attnT), ("ug", uT))]

            def up(t, groups):
                for group in groups:
                    r, k2, m = group // 4, group // 2 % 2, 1 - group % 2
                    if group % 4 == 0 and t == 0 and r < 2:
                        pe.wait_ge(piece_saved, PIECES - 1 + r)
                    if group % 4 == 0 and t == 1:
                        if r < 2:
                            pe.wait_ge(merged, KC // 2)
                        elif r == 2:
                            pe.wait_ge(var_ready, 3)
                    w, src = ups[m]
                    n = 2 * r + k2
                    for k in range(WC):
                        if (t, group, k) == (0, 1, WC - 1):
                            pe.wait_ge(attn_saved, WC)
                        last = T.matmul(bank[UP_BANKS[t][r]][:, (2 * k2 + m) * P:(2 * k2 + m + 1) * P],
                                        w[:, k, n * P:(n + 1) * P], src[:, k, t * P:(t + 1) * P],
                                        start=(k == 0), stop=(k == WC - 1))
                    if group % 4 == 3:
                        last.then_inc(up_ready, 1)

            def project(t):
                for m in range(2):
                    arrived(("o", m))
                    w = slot(("o", m)).rearrange("p (k n) -> p k n", k=KC)
                    for k in range(KC):
                        if m == 0 and k % 2 == 0:
                            pe.wait_ge(merged, KC // 2 * t + k // 2 + 1)
                        last = T.matmul(bank[OUT_BANKS[t][m]][:], hT[:, k, t * P:(t + 1) * P], w[:, k, :],
                                        start=(k == 0), stop=(k == KC - 1))
                    last.then_inc(o_ready, 1)

            def transpose_h(t):
                for k in range(KC):
                    if k % (KC // 2) == 0:
                        pe.wait_ge(h2_ready, 2 * t + k // (KC // 2) + 1)
                    last = T.transpose(bank[HT_BANKS[k // 4]][:, k % 4 * P:(k % 4 + 1) * P], h_sb[:, t, k * P:(k + 1) * P], ident[:])
                last.then_inc(h2T_ready, 1)

            def retrieve(p, t, filler=None):
                h = p - HEADS * t
                if isinstance(p, int) and p == 0:
                    for m in range(2):
                        for k in range(KC):
                            last = T.matmul(bank[QT_BANK][:, m * P:(m + 1) * P], wpq[:, k * 256 + m * P:k * 256 + (m + 1) * P],
                                            hT[:, k, t * P:(t + 1) * P], start=(k == 0), stop=(k == KC - 1))
                else:
                    for k in range(KC):
                        last = T.matmul(bank[Q_BANK][:, 0:256], hT[:, k, t * P:(t + 1) * P],
                                        wpq[:, bass.ds((h * KC + k) * 256, 256)], start=(k == 0), stop=(k == KC - 1))
                    last.then_inc(q_ready, 1)
                    pe.wait_ge(q_saved, p)
                    for m in range(2):
                        last = T.transpose(bank[QT_BANK][:, m * P:(m + 1) * P], q_tok[:, m * P:(m + 1) * P], ident[:])
                last.then_inc(qT_ready, 1)
                if filler is not None:
                    filler()
                pe.wait_ge(qT_saved, p + 1)
                for m in range(2):
                    last = T.matmul(bank[QT_BANK][:, (2 + m) * P:(3 + m) * P], qTs[:, m, :],
                                    keysT[:].rearrange("p m n -> p (m n)")[:, bass.ds((2 * h + m) * NKEYS, NKEYS)],
                                    start=True, stop=True)
                last.then_inc(s_ready, 1)

            def clear(t):
                for m in range(2):
                    last = T.matmul(bank[ACC_BANKS[t][m]][:, 0:BLK], zeros, h_sb[:, t, m * BLK:(m + 1) * BLK], start=True,
                                    stop=False, skip_group_check=True)
                return last

            def add_rows(i, a, t, following=None):
                p = 2 * i + a
                if following is not None:
                    pe.wait_ge(s_saved, p + 1)
                    retrieve(p + 1, following)
                for g in range(2):
                    n = 2 * p + g
                    rows = PE_ROWS if (following, g) == (None, 1) else range(GROUP)
                    for i, e in enumerate(rows):
                        pe.wait_ge(v_in[e], 16 * (n + 1))
                        pe.wait_ge(diag_ready, GROUP * n + i + 1)
                        end = isinstance(p, int) and p % HEADS == HEADS - 1 and (g, i) == (1, len(rows) - 1)
                        for m in range(2):
                            last = T.matmul(bank[ACC_BANKS[t][m]][:], diag[:, e, :], v_ring[e][:, m * BLK:(m + 1) * BLK],
                                            start=False, stop=end, skip_group_check=True)
                            if end and following is None:
                                last.then_inc(acc_ready, 1)
                        if not (end and following is None):
                            last.then_inc(v_used, 1)

            zeros = zero_tile[:]
            arrived(("ua", 0))
            arrived(("ug", 0))
            pe.wait_ge(gate_saved, 2)
            pe.wait_ge(attn_saved, WC - 1)
            up(0, range(16))
            project(0)
            up(1, range(14))
            transpose_h(0)
            up(1, [14])
            pe.wait_ge(h2T_saved, 2)
            pe.wait_ge(wpq_in[0], 16 * EARLY)
            retrieve(0, 0, filler=lambda: up(1, [15]))
            project(1)
            clear(0).then_inc(v_used, GROUP)
            add_rows(0, 0, 0, following=0)
            add_rows(0, 1, 0, following=0)
            transpose_h(1)
            clear(1)
            pe.wait_ge(wpq_in[1], 16 * (HEADS - EARLY))
            with pe.Fori(1, HEADS // 2 - 1) as i:
                add_rows(i, 0, 0, following=0)
                add_rows(i, 1, 0, following=0)
            pe.wait_ge(h2T_saved, 4)
            add_rows(HEADS // 2 - 1, 0, 0, following=0)
            add_rows(HEADS // 2 - 1, 1, 0, following=1)
            with pe.Fori(HEADS // 2, PAIRS // 2 - 1) as i:
                add_rows(i, 0, 1, following=1)
                add_rows(i, 1, 1, following=1)
            add_rows(PAIRS // 2 - 1, 0, 1, following=1)
            add_rows(PAIRS // 2 - 1, 1, 1)


_INS = ['x', 'c', 'w_cond', 'b_cond', 'w_in', 'w_attn_up', 'w_gmlp_up', 'w_out', 'sgu_ln_g', 'sgu_ln_b',
        'w_spatial', 'b_spatial', 'ln1_g', 'ln1_b', 'w_peer_q', 'peer_sub_keys', 'peer_u', 'peer_v', 'ln2_g', 'ln2_b']


def kernel(**inputs):
    import numpy as _np
    import concourse.bacc as _bacc
    from concourse import mybir as _mybir
    from concourse.bass_utils import run_bass_kernel_spmd as _run

    nc = _bacc.Bacc("TRN2", target_bir_lowering=False, num_devices=1)
    arrays, args = {}, []
    for name in _INS:
        a = _np.ascontiguousarray(inputs[name])
        arrays[f"in_{name}_dram"] = a
        args.append(nc.dram_tensor(f"in_{name}_dram", a.shape, _mybir.dt.from_np(a.dtype), kind="ExternalInput").ap())
    out = nc.dram_tensor("out_0_dram", (1, SEQ, D), F32, kind="ExternalOutput").ap()
    build(nc, *args, out)
    r = _run(nc, [arrays], core_ids=[0])
    return r.results[0]["out_0_dram"]
```
